# Optimizing a Trainium2 kernel written in Bass

```python
import jax, jax.numpy as jnp
from jax import lax
import numpy as np

D_MODEL = 2048
BATCH = 1
SEQ = 512
DEPTH = 2

N_MIXERS = 2
N_A_LAYERS = (DEPTH + 1) // 2
N_B_LAYERS = DEPTH // 2
EPS = 1e-6

EXPAND = 2
CHUNK = 128
A_WIDTH = EXPAND * D_MODEL
A_GROUPS = 16
A_GROUP_DIM = A_WIDTH // A_GROUPS

B_HEAD_DIM = 128
B_HEADS = D_MODEL // B_HEAD_DIM
B_WIDTH = B_HEADS * B_HEAD_DIM
Q_BLOCK = 128
FORGET_BIAS_MEAN = 3.0

kernel_name = "hybrid_gmlp_fox_interleaved"

def rms_norm(x, g):
    xf = x.astype(jnp.float32)
    y = xf * lax.rsqrt(jnp.mean(xf * xf, axis=-1, keepdims=True) + EPS)
    return (y * g.astype(jnp.float32)).astype(x.dtype)

def spatial_gating_layer(x, norm_g, w_in, v_norm_g, w_s, b_s, w_out):
    b, s, _ = x.shape
    h = rms_norm(x, norm_g)
    u, v, z = jnp.split(h @ w_in, 3, axis=-1)
    u = jax.nn.gelu(u)
    v = rms_norm(jax.nn.gelu(v), v_norm_g)
    n_chunks = s // CHUNK
    v = v.reshape(b, n_chunks, CHUNK, A_GROUPS, A_GROUP_DIM)
    causal = jnp.tril(jnp.ones((CHUNK, CHUNK), dtype=bool))
    w_causal = jnp.where(causal[None], w_s, 0)
    mixed = jnp.einsum('gts,bcsgd->bctgd', w_causal, v) + b_s.T[None, None, :, :, None]
    mixed = mixed.reshape(b, s, A_WIDTH)
    y = u * mixed * jax.nn.silu(z)
    return y @ w_out

def forgetting_attention_layer(x, norm_g, w_in, f_bias, q_norm_g, k_norm_g, w_out):
    b, s, _ = x.shape
    h = rms_norm(x, norm_g)
    proj = h @ w_in
    q, k, v, z, f_logit = jnp.split(
        proj, [B_WIDTH, 2 * B_WIDTH, 3 * B_WIDTH, 4 * B_WIDTH], axis=-1)
    q = rms_norm(q.reshape(b, s, B_HEADS, B_HEAD_DIM), q_norm_g)
    k = rms_norm(k.reshape(b, s, B_HEADS, B_HEAD_DIM), k_norm_g)
    v = v.reshape(b, s, B_HEADS, B_HEAD_DIM)
    log_f = jax.nn.log_sigmoid((f_logit + f_bias).astype(jnp.float32))
    cum = jnp.cumsum(log_f, axis=1).transpose(0, 2, 1)
    scale = B_HEAD_DIM ** -0.5
    q_t = q.transpose(0, 2, 1, 3)
    k_t = k.transpose(0, 2, 1, 3)
    v_t = v.transpose(0, 2, 1, 3)
    n_blocks = s // Q_BLOCK
    q_blocks = q_t.reshape(b, B_HEADS, n_blocks, Q_BLOCK, B_HEAD_DIM).transpose(2, 0, 1, 3, 4)
    c_blocks = cum.reshape(b, B_HEADS, n_blocks, Q_BLOCK).transpose(2, 0, 1, 3)
    blk_idx = jnp.arange(n_blocks, dtype=jnp.int32)
    k_pos = jnp.arange(s, dtype=jnp.int32)

    def attend_block(args):
        q_blk, c_blk, i = args
        logits = jnp.einsum('bhqd,bhkd->bhqk', q_blk, k_t,
                            preferred_element_type=jnp.float32) * scale
        logits = logits + c_blk[..., :, None] - cum[:, :, None, :]
        q_pos = i * Q_BLOCK + jnp.arange(Q_BLOCK, dtype=jnp.int32)
        mask = k_pos[None, :] <= q_pos[:, None]
        logits = jnp.where(mask, logits, -jnp.inf)
        p = jax.nn.softmax(logits, axis=-1).astype(v_t.dtype)
        return jnp.einsum('bhqk,bhkd->bhqd', p, v_t)

    out = lax.map(attend_block, (q_blocks, c_blocks, blk_idx))
    out = out.transpose(1, 0, 3, 2, 4).reshape(b, s, B_WIDTH)
    y = out * jax.nn.silu(z)
    return y @ w_out

def setup_inputs(seed: int = 0) -> dict:
    key = jax.random.key(seed)
    ks = jax.random.split(key, 13)
    f32 = jnp.float32
    x = jax.random.normal(ks[0], (BATCH, SEQ, D_MODEL), f32)
    a_norm_g = 1.0 + 0.05 * jax.random.normal(ks[1], (N_A_LAYERS, D_MODEL), f32)
    a_w_in = jax.random.normal(ks[2], (N_A_LAYERS, D_MODEL, 3 * A_WIDTH), f32) * D_MODEL ** -0.5
    a_v_norm_g = 1.0 + 0.05 * jax.random.normal(ks[3], (N_A_LAYERS, A_WIDTH), f32)
    a_w_s = jax.random.normal(ks[4], (N_A_LAYERS, A_GROUPS, CHUNK, CHUNK), f32) * CHUNK ** -0.5
    a_b_s = 1.0 + 0.1 * jax.random.normal(ks[5], (N_A_LAYERS, A_GROUPS, CHUNK), f32)
    a_w_out = jax.random.normal(ks[6], (N_A_LAYERS, A_WIDTH, D_MODEL), f32) * A_WIDTH ** -0.5
    b_norm_g = 1.0 + 0.05 * jax.random.normal(ks[7], (N_B_LAYERS, D_MODEL), f32)
    b_w_in = jax.random.normal(ks[8], (N_B_LAYERS, D_MODEL, 4 * B_WIDTH + B_HEADS), f32) * D_MODEL ** -0.5
    b_f_bias = FORGET_BIAS_MEAN + 0.5 * jax.random.normal(ks[9], (N_B_LAYERS, B_HEADS), f32)
    b_q_norm_g = 1.0 + 0.05 * jax.random.normal(ks[10], (N_B_LAYERS, B_HEAD_DIM), f32)
    b_k_norm_g = 1.0 + 0.05 * jax.random.normal(ks[11], (N_B_LAYERS, B_HEAD_DIM), f32)
    b_w_out = jax.random.normal(ks[12], (N_B_LAYERS, B_WIDTH, D_MODEL), f32) * B_WIDTH ** -0.5
    return {"x": x, "a_norm_g": a_norm_g, "a_w_in": a_w_in, "a_v_norm_g": a_v_norm_g,
            "a_w_s": a_w_s, "a_b_s": a_b_s, "a_w_out": a_w_out,
            "b_norm_g": b_norm_g, "b_w_in": b_w_in, "b_f_bias": b_f_bias,
            "b_q_norm_g": b_q_norm_g, "b_k_norm_g": b_k_norm_g, "b_w_out": b_w_out}

def reference(x, a_norm_g, a_w_in, a_v_norm_g, a_w_s, a_b_s, a_w_out,
              b_norm_g, b_w_in, b_f_bias, b_q_norm_g, b_k_norm_g, b_w_out):
    for i in range(DEPTH):
        j = i // N_MIXERS
        if i % N_MIXERS == 0:
            x = x + spatial_gating_layer(x, a_norm_g[j], a_w_in[j], a_v_norm_g[j],
                                         a_w_s[j], a_b_s[j], a_w_out[j])
        else:
            x = x + forgetting_attention_layer(x, b_norm_g[j], b_w_in[j], b_f_bias[j],
                                               b_q_norm_g[j], b_k_norm_g[j], b_w_out[j])
    return x


_drawn_inputs = setup_inputs


def setup_inputs(seed=0):
    import zlib

    import numpy as np

    out = dict(_drawn_inputs(seed))
    spreads = {}
    factors = {'a_v_norm_g': 4.413, 'b_norm_g': 3.763, 'b_q_norm_g': 7.548, 'b_k_norm_g': 8.0}
    for name, (base, spread) in spreads.items():
        noise = np.random.default_rng([zlib.crc32(name.encode()), seed]).standard_normal(out[name].shape)
        drawn = base * np.exp(spread * noise) if base else spread * noise
        out[name] = __import__('jax').numpy.asarray(drawn.astype(out[name].dtype))
    for name, factor in factors.items():
        out[name] = (out[name] * factor).astype(out[name].dtype)
    return out
```

```python
from contextlib import ExitStack

import concourse.bass as bass
from concourse import mybir

F32 = mybir.dt.float32
F32R = mybir.dt.float32r
BF16 = mybir.dt.bfloat16
ACT = mybir.ActivationFunctionType
ALU = mybir.AluOpType
AX = mybir.AxisListType
ds = bass.ds

P = 128
EPS = 1e-6


def build_trunk(nc, x, a_norm_g, a_w_in, a_v_norm_g, a_w_s, a_b_s, a_w_out,
                b_norm_g, b_w_in, b_f_bias, b_q_norm_g, b_k_norm_g, b_w_out, out):
    SEQ, D = x.shape[1], x.shape[2]
    NT = SEQ // P
    KC = D // P
    AW = a_w_out.shape[1]
    G = a_w_s.shape[1]
    GD = AW // G
    H = b_f_bias.shape[1]
    HD = b_q_norm_g.shape[1]
    FB = 512
    NF = D // FB
    VB = AW // FB
    R = 4
    OK = GD // P
    assert (NT, NF, GD, HD, OK, SEQ) == (4, 4, 256, P, 2, 512) and G == H == 16 == KC
    OT = NF * OK
    SCALE = float(HD) ** -0.5
    NEG = -1e30

    A0 = VB * KC
    AL = A0 + KC
    APAIR = 2 * (KC + OT)
    AE = AL + (G // 2 - 1) * APAIR
    B0 = AE + KC + 2 * OT
    BL = B0 + KC
    BPAIR = 2 * KC + OT
    BE = BL + (H // 2 - 1) * BPAIR
    assert A0 % R == AL % R == APAIR % R == AE % R == B0 % R == BPAIR % R == 0

    x_t = x[0].rearrange("(t p) d -> p t d", p=P)
    out_t = out[0].rearrange("(t p) d -> p t d", p=P)
    a_in = a_w_in[0]
    a_uz = a_w_in[0].rearrange("r (s c) -> r s c", s=3)[:, 0:3:2, :]
    a_out = a_w_out[0]
    b_qkvz = b_w_in[0][:, 0:4 * D].rearrange("r (s c) -> r s c", s=4)
    b_f = b_w_in[0][:, 4 * D:4 * D + H].rearrange("(k p) h -> p k h", p=P)
    b_out = b_w_out[0]
    cum_dram = nc.dram_tensor("cum_rows", [H, SEQ], F32).ap()

    with ExitStack() as ctx:
        def sb(name, shape, dt=F32):
            return ctx.enter_context(nc.sbuf_tensor(name, shape, dt))

        def sem(name):
            return ctx.enter_context(nc.semaphore(name))

        acc = sb("acc", [P, NT, D])
        xh = sb("xh", [P, KC, SEQ], F32R)
        xl = sb("xl", [P, KC, SEQ], F32R)
        v_all = sb("v_all", [P, G * NT * GD])
        v = v_all[:, :].rearrange("p (g c d) -> p g c d", g=G, c=NT)
        yh = sb("yh", [P, OK, SEQ], F32R)
        yl = sb("yl", [P, OK, SEQ], F32R)
        ug = sb("ug", [P, NT, GD])
        zz = sb("zz", [P, NT, GD])
        w_raw = sb("w_raw", [P, R, FB])
        w_hi = sb("w_hi", [P, R, FB], F32R)
        w_lo = sb("w_lo", [P, R, FB], F32R)
        ident = sb("ident", [P, P])
        ident_b = sb("ident_b", [P, P], BF16)
        mask_b = sb("mask_b", [P, P], BF16)
        ws_raw = sb("ws_raw", [P, 2, P])
        ws_T = sb("ws_T", [P, P])
        vg_row = sb("vg_row", [P, 2, GD])
        rows = sb("rows", [2 * KC + G, P])
        cols = sb("cols", [P, 2 * KC + G])
        mhalf = sb("mhalf", [P, 2 * NT])
        ssx = sb("ssx", [P, NT])
        msx = sb("msx", [P, NT])
        rstd = sb("rstd", [P, NT])
        hrstd = sb("hrstd", [P, NT])
        vsq = sb("vsq", [P, NT, VB])
        vms = sb("vms", [P, 2, NT])
        vrstd = sb("vrstd", [P, NT])
        qkss = sb("qkss", [P, NT, 2])
        qkms = sb("qkms", [P, NT, 2])
        qkr = sb("qkr", [P, NT, 2])
        nmax = sb("nmax", [P, NT])
        rsum = sb("rsum", [P, NT])
        rinv = sb("rinv", [P, NT])

        a_gain, b_gain, b_s_cols = cols[:, 0:KC], cols[:, KC:2 * KC], cols[:, 2 * KC:]

        at = [0]

        def part(n, pattern=None, **sizes):
            ap = v_all[:, at[0]:at[0] + n]
            at[0] += n
            return ap.rearrange(pattern, **sizes) if pattern else ap

        qk = part(NT * 2 * HD, "p (t s d) -> p t s d", t=NT, s=2)
        vn = part(NT * HD, "p (t d) -> p t d", t=NT)
        zb = part(NT * HD, "p (t d) -> p t d", t=NT)
        yb = part(NT * HD, "p (t d) -> p t d", t=NT)
        qT = part(SEQ)
        kT = part(SEQ)
        NB = NT * (NT + 1) // 2
        probs = part(NB * P)
        probs_T = part(NB * P)
        cum_row = part(2 * SEQ, "p (b s) -> p b s", b=2)
        qg_row = part(HD)
        kg_row = part(HD)
        fb_row = part(H)
        wf_raw = part(KC * H)
        f_log = part(NT * H, "p (t h) -> p t h", t=NT)
        f_e = part(NT * H, "p (t h) -> p t h", t=NT)
        f_abs = part(NT * H, "p (t h) -> p t h", t=NT)
        f_T = part(SEQ)
        f_one = part(SEQ)
        cum_T = part(SEQ)
        cum_col = part(NT * H, "p (t h) -> p t h", t=NT)
        junk = part(D)
        row_at = [i * (i + 1) // 2 * P for i in range(NT + 1)]
        wf_hi, wf_lo = yh[:, 0, 0:KC * H], yl[:, 0, 0:KC * H]

        ps = [ctx.enter_context(nc.psum_tensor(f"ps{i}", [P, 4, 512], F32)) for i in range(2)]

        w_loaded = [sem(f"w_loaded{s}") for s in range(R)]
        hi_ready = sem("hi_ready")
        lo_ready = sem("lo_ready")
        tile_used = sem("tile_used")
        x_loaded = [sem(f"x_loaded{c}") for c in range(NF)]
        rows_loaded = sem("rows_loaded")
        const_ready = sem("const_ready")
        rows_T = sem("rows_T")
        cols_ready = sem("cols_ready")
        xT_ready = sem("xT_ready")
        xh_ready = sem("xh_ready")
        xl_ready = sem("xl_ready")
        ssx_ready = sem("ssx_ready")
        msx_ready = sem("msx_ready")
        rstd_ready = sem("rstd_ready")
        hrstd_ready = sem("hrstd_ready")
        v_out = sem("v_out")
        vsq_ready = sem("vsq_ready")
        vms_ready = sem("vms_ready")
        vrstd_ready = sem("vrstd_ready")
        ws_loaded = [sem("ws_loaded0"), sem("ws_loaded1")]
        vg_loaded = [sem("vg_loaded0"), sem("vg_loaded1")]
        mask_turn = sem("mask_turn")
        ws_masked = sem("ws_masked")
        ws_T_psum = sem("ws_T_psum")
        ws_T_ready = sem("ws_T_ready")
        v_normed = sem("v_normed")
        mixed = sem("mixed")
        mix_ready = sem("mix_ready")
        u_ready = sem("u_ready")
        tanh_ready = sem("tanh_ready")
        block_out = sem("block_out")
        gate_step = sem("gate_step")
        y_ready = sem("y_ready")
        yT_psum = sem("yT_psum")
        yh_ready = sem("yh_ready")
        yl_ready = sem("yl_ready")
        sum_out = sem("sum_out")
        heads_out = sem("heads_out")
        qk_out = sem("qk_out")
        tanh_b = sem("tanh_b")
        v_b = sem("v_b")
        qkss_ready = sem("qkss_ready")
        qkms_ready = sem("qkms_ready")
        qkr_ready = sem("qkr_ready")
        qkr_scaled = sem("qkr_scaled")
        qk_normed = sem("qk_normed")
        qkT_psum = sem("qkT_psum")
        qT_ready = sem("qT_ready")
        kT_ready = sem("kT_ready")
        scores = sem("scores")
        logits = sem("logits")
        nmax_ready = sem("nmax_ready")
        probs_ready = sem("probs_ready")
        rinv_ready = sem("rinv_ready")
        probsT_psum = sem("probsT_psum")
        probsT_act = sem("probsT_act")
        probsT_dve = sem("probsT_dve")
        attended = sem("attended")
        yb_ready = sem("yb_ready")
        gains_loaded = sem("gains_loaded")
        gains_ready = sem("gains_ready")
        wf_loaded = sem("wf_loaded")
        wf_hi_ready = sem("wf_hi_ready")
        wf_lo_ready = sem("wf_lo_ready")
        f_psum = sem("f_psum")
        f_step = sem("f_step")
        f_act = sem("f_act")
        fT_psum = sem("fT_psum")
        cumT_ready = sem("cumT_ready")
        cum_stored = sem("cum_stored")
        cumc_psum = sem("cumc_psum")
        cumc_ready = sem("cumc_ready")
        cum_loaded = [sem("cum_loaded0"), sem("cum_loaded1")]
        out_stored = sem("out_stored")

        block = ctx.enter_context(nc.Block())

        @block.sync
        def _(sp):
            def load(n, i, src, first=False):
                s = i % R
                if not first:
                    sp.wait_ge(lo_ready, n + (i - R + 1))
                dst = w_raw[:, s, :]
                if len(src.shape) == 3:
                    dst = dst.rearrange("p (s c) -> p s c", s=src.shape[1])
                sp.dma_start(dst, src).then_inc(w_loaded[s], 16)

            def v_block(n, b, first=False):
                for k in range(KC):
                    load(n, k, a_in[k * P:(k + 1) * P, ds(AW + b * FB, FB)], first and k < R)

            def a_block(n, off, g):
                for k in range(KC):
                    load(n, off + k, a_uz[k * P:(k + 1) * P, :, ds(g * GD, GD)])

            def out_proj(n, off, w, row):
                for f in range(NF):
                    for k in range(OK):
                        load(n, off + f * OK + k, w[ds(row + k * P, P), f * FB:(f + 1) * FB])

            def b_block(n, off, h):
                for k in range(KC):
                    load(n, off + k, b_qkvz[k * P:(k + 1) * P, :, ds(h * HD, HD)])

            v_block(0, 0, first=True)
            v_block(KC, 1)
            with sp.Fori(1, VB // 2) as j:
                v_block(j * (2 * KC), j * 2)
                v_block(j * (2 * KC) + KC, j * 2 + 1)
            a_block(A0, 0, 0)
            with sp.Fori(0, G // 2 - 1) as j:
                n = j * APAIR + AL
                a_block(n, 0, j * 2 + 1)
                out_proj(n, KC, a_out, j * (2 * GD))
                a_block(n, KC + OT, j * 2 + 2)
                out_proj(n, 2 * KC + OT, a_out, j * (2 * GD) + GD)
            a_block(AE, 0, G - 1)
            out_proj(AE, KC, a_out, (G - 2) * GD)
            out_proj(AE, KC + OT, a_out, (G - 1) * GD)
            b_block(B0, 0, 0)
            with sp.Fori(0, H // 2 - 1) as j:
                n = j * BPAIR + BL
                b_block(n, 0, j * 2 + 1)
                b_block(n, KC, j * 2 + 2)
                out_proj(n, 2 * KC, b_out, j * (2 * HD))
            b_block(BE, 0, H - 1)
            out_proj(BE, KC, b_out, (H - 2) * HD)
            for f in range(NF):
                sp.wait_ge(sum_out, NF * (1 + G + H // 2 - 1) + f + 1)
                sp.dma_start(out_t[:, :, f * FB:(f + 1) * FB],
                             acc[:, :, f * FB:(f + 1) * FB]).then_inc(out_stored, 16)
            sp.wait_ge(out_stored, 16 * NF)

        @block.gpsimd
        def _(pool):
            pool.memset(ident[:, :], 0.0).then_inc(const_ready, 1)
            pool.memset(ident_b[:, :], 0.0).then_inc(const_ready, 1)
            pool.memset(mask_b[:, :], 0.0).then_inc(const_ready, 1)
            pool.memset(mhalf[:, :], -0.5).then_inc(const_ready, 1)
            pool.wait_ge(const_ready, 4)
            for m in (ident, ident_b):
                pool.affine_select(out=m[:, :], in_=m[:, :], compare_op=ALU.not_equal, fill=1.0,
                                   base=0, pattern=[[-1, P]], channel_multiplier=1).then_inc(const_ready, 1)
            pool.affine_select(out=mask_b[:, :], in_=mask_b[:, :], compare_op=ALU.is_ge, fill=NEG,
                               base=0, pattern=[[-1, P]], channel_multiplier=1).then_inc(const_ready, 1)

            def power(dst, src, n):
                return pool.tensor_tensor(dst, src, mhalf[:, 0:n], ALU.pow)

            pool.wait_ge(msx_ready, 1)
            power(rstd[:, :], msx[:, :], NT).then_inc(rstd_ready, 1)

            def load_group(g, s, first=False):
                if not first:
                    pool.wait_ge(ws_T_psum, g - 1)
                    pool.wait_ge(v_normed, g - 1)
                pool.dma_start(ws_raw[:, s, :], a_w_s[0, ds(g, 1)].rearrange("a t s -> t (a s)"))\
                    .then_inc(ws_loaded[s], 16)
                pool.dma_start(vg_row[:, s, :], a_v_norm_g[0:1, ds(g * GD, GD)].broadcast_to([P, GD]))\
                    .then_inc(vg_loaded[s], 16)

            def mask_group(g, s, count):
                pool.wait_ge(ws_loaded[s], count)
                pool.sem_inc(mask_turn, 1)
                pool.affine_select(out=ws_raw[:, s, :], in_=ws_raw[:, s, :], compare_op=ALU.is_ge,
                                   fill=0.0, base=0, pattern=[[-1, P]], channel_multiplier=1)\
                    .then_inc(ws_masked, 1)

            load_group(0, 0, first=True)
            load_group(1, 1, first=True)
            mask_group(0, 0, 16)
            pool.wait_ge(vms_ready, 2)
            power(vrstd[:, :], vms[:, 1, :], NT).then_inc(vrstd_ready, 1)
            mask_group(1, 1, 16)
            with pool.Fori(1, G // 2) as j:
                for s in range(2):
                    load_group(j * 2 + s, s)
                    mask_group(j * 2 + s, s, j * 16 + 16)

            pool.wait_ge(y_ready, G)
            pool.dma_start(qg_row, b_q_norm_g[0:1, :].broadcast_to([P, HD])).then_inc(gains_loaded, 16)
            pool.dma_start(kg_row, b_k_norm_g[0:1, :].broadcast_to([P, HD])).then_inc(gains_loaded, 16)
            pool.dma_start(fb_row, b_f_bias[0:1, :].broadcast_to([P, H])).then_inc(gains_loaded, 16)
            pool.dma_start(wf_raw.rearrange("p (k h) -> p k h", h=H), b_f).then_inc(wf_loaded, 16)
            pool.memset(f_one[0:H, :], 1.0).then_inc(const_ready, 1)
            pool.wait_ge(msx_ready, 2)
            pool.wait_ge(hrstd_ready, 1)
            power(rstd[:, :], msx[:, :], NT).then_inc(rstd_ready, 1)
            pool.wait_ge(cumT_ready, 1)
            pool.dma_start(cum_dram, cum_T[0:H, :]).then_inc(cum_stored, 16)
            pool.wait_ge(cum_stored, 16)

            def load_cum(h, s, first=False):
                if not first:
                    pool.wait_ge(logits, (h - 1) * NT)
                pool.dma_start(cum_row[:, s, :], cum_dram[ds(h, 1), :].broadcast_to([P, SEQ]))\
                    .then_inc(cum_loaded[s], 16)

            def head_power(h):
                pool.wait_ge(qkms_ready, h + 1)
                power(qkr[:, :, :], qkms[:, :, :], 2 * NT).then_inc(qkr_ready, 1)

            load_cum(0, 0, first=True)
            load_cum(1, 1, first=True)
            head_power(0)
            head_power(1)
            with pool.Fori(1, H // 2) as j:
                for s in range(2):
                    load_cum(j * 2 + s, s)
                    head_power(j * 2 + s)

        @block.scalar
        def _(act):
            for r, src in ((0, a_norm_g[0].rearrange("(k p) -> k p", p=P)),
                           (KC, b_norm_g[0].rearrange("(k p) -> k p", p=P)), (2 * KC, a_b_s[0])):
                act.dma_start(rows[r:r + src.shape[0], :], src).then_inc(rows_loaded, 16)
            for c in range(NF):
                act.dma_start(acc[:, :, c * FB:(c + 1) * FB],
                              x_t[:, :, c * FB:(c + 1) * FB]).then_inc(x_loaded[c], 16)

            def split(n, i, loads, first=False):
                s = i % R
                act.wait_ge(w_loaded[s], loads * 16)
                if not first:
                    act.wait_ge(tile_used, n + (i - R + 1))
                act.activation(w_hi[:, s, :], w_raw[:, s, :], ACT.Copy).then_inc(hi_ready, 1)

            def loads_of(first_tile, i):
                return first_tile // R + i // R + 1

            def x_high(k, gain, done):
                act.wait_ge(xT_ready, done + k + 1)
                act.activation(xh[:, k, :], ps[1][:, k % 4, :], ACT.Copy,
                               scale=gain[:, k:k + 1]).then_inc(xh_ready, 1)

            act.wait_ge(cols_ready, 1)
            for k in range(4):
                x_high(k, a_gain, 0)
            for k in range(KC):
                split(0, k, loads_of(0, k), first=k < R)
                if k + 4 < KC:
                    x_high(k + 4, a_gain, 0)
            for t in range(NT):
                act.activation(junk, acc[:, t, :], ACT.Square, accum_out=ssx[:, t:t + 1])\
                    .then_inc(ssx_ready, 1)
                act.wait_ge(ssx_ready, t + 1)

            def v_leave(n, i, S, b):
                act.wait_ge(tile_used, n + i)
                for t in range(NT):
                    dst = v[:, ds(b * 2, 2), t, :]
                    act.activation(dst, ps[S][:, t, :].rearrange("p (g d) -> p g d", g=2),
                                   ACT.Gelu_apprx_tanh, scale=rstd[:, t:t + 1]).then_inc(v_out, 1)
                for t in range(NT):
                    act.wait_ge(v_out, b * NT + (t + 1))
                    if t == 0:
                        act.wait_ge(vsq_ready, b * NT)
                    act.activation((ug, zz)[t // 2][:, t % 2 * 2:t % 2 * 2 + 2, :], v[:, ds(b * 2, 2), t, :], ACT.Square,
                                   accum_out=vsq[:, t, ds(b, 1)]).then_inc(vsq_ready, 1)

            def v_block(n, q, b, S, wait_rstd=False):
                for k in range(KC):
                    split(n, k, q + (k // R + 1))
                    if k == 2:
                        if wait_rstd:
                            act.wait_ge(rstd_ready, 1)
                        v_leave(n, 0, S, b - 1)

            v_block(KC, KC // R, 1, 0, wait_rstd=True)
            with act.Fori(1, VB // 2) as j:
                v_block(j * (2 * KC), j * (2 * KC // R), j * 2, 1)
                v_block(j * (2 * KC) + KC, j * (2 * KC // R) + KC // R, j * 2 + 1, 0)

            def leave(n, i, g, S):
                act.wait_ge(tile_used, n + i)
                act.wait_ge(y_ready, g)
                act.wait_ge(yT_psum, g)
                for t in range(NT):
                    ins = act.activation(ug[:, t, :], ps[S][:, t, 0:GD], ACT.Gelu_apprx_tanh,
                                         scale=rstd[:, t:t + 1])
                ins.then_inc(u_ready, 1)
                for t in range(NT):
                    ins = act.activation(zz[:, t, :], ps[S][:, t, GD:2 * GD], ACT.Tanh,
                                         scale=hrstd[:, t:t + 1])
                ins.then_inc(tanh_ready, 1)

            def y_high(O, count):
                act.wait_ge(yT_psum, count)
                act.activation(yh[:, :, :], ps[O][:, 0:OK, :], ACT.Copy).then_inc(yh_ready, 1)

            for k in range(KC):
                split(A0, k, A0 // R + k // R + 1)
                if k == 2:
                    v_leave(A0, 0, 1, VB - 1)
            act.wait_ge(hrstd_ready, 1)

            def a_block(n, q, off, g, S):
                for k in range(KC):
                    split(n, off + k, q + ((off + k) // R + 1))
                    if k == 5:
                        y_high(1 - S, g)

            def out_tiles(n, q, off):
                for i in range(OT):
                    split(n, off + i, q + ((off + i) // R + 1))
                    if i == 2:
                        yield

            def a_out_tiles(n, q, off, g, S):
                for i in range(OT):
                    split(n, off + i, q + ((off + i) // R + 1))
                    if i == 2:
                        leave(n, off, g, S)

            def a_block1(n, q, off, g, S, leave_first):
                for k in range(KC):
                    split(n, off + k, q + ((off + k) // R + 1))
                    if k == 5:
                        y_high(1 - S, g)

            leave(A0, KC, 0, 0)
            with act.Fori(0, G // 2 - 1) as j:
                n, q = j * APAIR + AL, j * (APAIR // R) + AL // R
                a_block(n, q, 0, j * 2 + 1, 1)
                a_out_tiles(n, q, KC, j * 2 + 1, 1)
                a_block(n, q, KC + OT, j * 2 + 2, 0)
                a_out_tiles(n, q, 2 * KC + OT, j * 2 + 2, 0)
            q = AE // R
            a_block(AE, q, 0, G - 1, 1)
            a_out_tiles(AE, q, KC, G - 1, 1)
            y_high(0, G)
            for i in range(OT):
                split(AE, KC + OT + i, q + (KC + OT + i) // R + 1)

            for k in range(4):
                x_high(k, b_gain, KC)
            for k in range(KC):
                split(B0, k, (B0 + k) // R + 1)
                if k + 4 < KC:
                    x_high(k + 4, b_gain, KC)
            act.wait_ge(gains_loaded, 48)
            for t in range(NT):
                act.activation(junk, acc[:, t, :], ACT.Square, accum_out=ssx[:, t:t + 1])\
                    .then_inc(ssx_ready, 1)
                act.wait_ge(ssx_ready, NT + t + 1)
            act.wait_ge(wf_loaded, 16)
            act.activation(wf_hi, wf_raw, ACT.Copy).then_inc(wf_hi_ready, 1)
            act.wait_ge(rstd_ready, 2)

            def head_leave(n, i, h, S):
                act.wait_ge(tile_used, n + i)
                act.wait_ge(yb_ready, h)
                for t in range(NT):
                    ins = act.activation(zb[:, t, :], ps[S][:, t, 3 * HD:4 * HD], ACT.Tanh,
                                         scale=hrstd[:, t:t + 1])
                ins.then_inc(tanh_b, 1)
                for t in range(NT):
                    ins = act.activation(vn[:, t, :], ps[S][:, t, 2 * HD:3 * HD], ACT.Copy,
                                         scale=rstd[:, t:t + 1])
                ins.then_inc(v_b, 1)
                act.wait_ge(qk_out, h + 1)
                act.wait_ge(probsT_psum, h)
                for t in range(NT):
                    for s in range(2):
                        ins = act.activation(probs[:, (2 * t + s) * P:(2 * t + s + 1) * P], qk[:, t, s, :],
                                             ACT.Square, scale=rstd[:, t:t + 1],
                                             accum_out=qkss[:, t, s:s + 1])
                ins.then_inc(qkss_ready, 1)

            def exps(h):
                for i in range(NT):
                    act.wait_ge(nmax_ready, h * NT + (i + 1))
                    act.activation(probs[:, row_at[i]:row_at[i + 1]], probs[:, row_at[i]:row_at[i + 1]],
                                   ACT.Exp, bias=nmax[:, i:i + 1], accum_out=rsum[:, i:i + 1])\
                        .then_inc(probs_ready, 1)

            def head_steps(k, h, O):
                if k == 5:
                    act.wait_ge(qkT_psum, h * 2 + 1)
                    act.activation(qT, ps[O][:, 0, :], ACT.Copy).then_inc(qT_ready, 1)
                elif k == 8:
                    exps(h)
                elif k == 11:
                    act.wait_ge(probsT_psum, h + 1)
                    act.activation(probs_T[:, 0:8 * P].rearrange("p (b c) -> p b c", b=2),
                                   ps[O][:, 0:2, :], ACT.Copy).then_inc(probsT_act, 1)
                elif k == 15:
                    act.wait_ge(yT_psum, h + (G + 1))
                    act.activation(yh[:, h_slot[0], :], ps[O][:, 0, :], ACT.Copy).then_inc(yh_ready, 1)

            h_slot = [0]

            def b_block(n, q, off, h, S, prev_out=False):
                for k in range(KC):
                    split(n, off + k, q + ((off + k) // R + 1))
                    if k == 2 and prev_out:
                        head_leave(n, off, h - 1, 1 - S)
                    head_steps(k, h - 1, 1 - S)

            act.wait_ge(f_step, 3)
            act.activation(f_e[:, :, :], f_abs[:, :, :], ACT.Exp, scale=-1.0).then_inc(f_act, 1)
            act.wait_ge(f_act, 1)
            act.activation(f_abs[:, :, :], f_e[:, :, :], ACT.Ln, bias=1.0).then_inc(f_act, 1)
            head_leave(B0, KC, 0, 0)
            with act.Fori(0, H // 2 - 1) as j:
                n, q = j * BPAIR + BL, j * (BPAIR // R) + BL // R
                h_slot[0] = 0
                b_block(n, q, 0, j * 2 + 1, 1)
                h_slot[0] = 1
                b_block(n, q, KC, j * 2 + 2, 0, prev_out=True)
                for i in range(OT):
                    split(n, 2 * KC + i, q + ((2 * KC + i) // R + 1))
                    if i == 2:
                        head_leave(n, 2 * KC, j * 2 + 2, 0)
            h_slot[0] = 0
            b_block(BE, BE // R, 0, H - 1, 1)
            for i in range(3):
                split(BE, KC + i, (BE + KC + i) // R + 1)
            head_leave(BE, KC, H - 1, 1)
            h_slot[0] = 1
            for k in (5, 8, 11, 15):
                head_steps(k, H - 1, 0)
            for i in range(3, OT):
                split(BE, KC + i, (BE + KC + i) // R + 1)

        @block.tensor
        def _(pe):
            def tile(n, i, S, hi, lo, start, stop):
                s = i % R
                pe.wait_ge(lo_ready, n + (i + 1))
                for t in range(NT):
                    a, b = hi[:, t * P:(t + 1) * P], lo[:, t * P:(t + 1) * P]
                    pe.matmul(ps[S][:, t, :], a, w_hi[:, s, :], start=start, stop=False)
                    pe.matmul(ps[S][:, t, :], a, w_lo[:, s, :], start=False, stop=False)
                    mm = pe.matmul(ps[S][:, t, :], b, w_hi[:, s, :], start=False, stop=stop)
                mm.then_inc(tile_used, 1)

            def in_tile(n, i, k, S):
                tile(n, i, S, xh[:, k, :], xl[:, k, :], k == 0, k == KC - 1)

            def turn_x(k, done):
                if k >= 4:
                    pe.wait_ge(xl_ready, done + k - 3)
                for t in range(NT):
                    mm = pe.transpose(ps[1][:, k % 4, t * P:(t + 1) * P],
                                      acc[:, t, k * P:(k + 1) * P], ident[:, :])
                mm.then_inc(xT_ready, 1)

            pe.wait_ge(const_ready, 7)
            pe.wait_ge(rows_loaded, 48)
            pe.transpose(ps[0][:, 0, 0:2 * KC + G], rows[:, :], ident[0:2 * KC + G, 0:2 * KC + G])\
                .then_inc(rows_T, 1)
            for k in range(4):
                pe.wait_ge(x_loaded[0], 16)
                turn_x(k, 0)
            pe.wait_ge(cols_ready, 1)
            for k in range(KC):
                pe.wait_ge(xl_ready, k + 1)
                in_tile(0, k, k, 0)
                if k + 4 < KC:
                    if k % 4 == 0:
                        pe.wait_ge(x_loaded[k // 4 + 1], 16)
                    turn_x(k + 4, 0)
            pe.wait_ge(xl_ready, KC)
            for k in range(KC):
                in_tile(KC, k, k, 1)
            with pe.Fori(1, VB // 2) as j:
                for S in range(2):
                    pe.wait_ge(v_out, j * (2 * NT) + (S * NT - NT))
                    for k in range(KC):
                        in_tile(j * (2 * KC), S * KC + k, k, S)

            def turn_ws(g, s, O):
                pe.wait_ge(ws_masked, g + 1)
                pe.transpose(ps[O][:, 3, 0:P], ws_raw[:, s, :], ident[:, :]).then_inc(ws_T_psum, 1)

            def turn_y(O, count):
                pe.wait_ge(y_ready, count)
                for c in range(OK):
                    for t in range(NT):
                        mm = pe.transpose(ps[O][:, c, t * P:(t + 1) * P],
                                          ug[:, t, c * P:(c + 1) * P], ident[:, :])
                mm.then_inc(yT_psum, 1)

            def mix(g, O):
                pe.wait_ge(ws_T_ready, g + 1)
                pe.wait_ge(v_normed, g + 1)
                for c in range(2):
                    mm = pe.matmul(ps[O][:, 2 + c, :], ws_T[:, :],
                                   v[:, ds(g, 1), 2 * c:2 * c + 2, :].rearrange("p g c d -> p (g c d)"),
                                   start=True, stop=True)
                mm.then_inc(mixed, 1)

            def a_block(n, off, g, S):
                O = 1 - S
                pe.wait_ge(sum_out, g * NF - 1)
                pe.wait_ge(mix_ready, g)
                for k in range(KC):
                    in_tile(n, off + k, k, S)
                    if k == 3:
                        pe.wait_ge(sum_out, g * NF)
                        pe.wait_ge(block_out, g)
                        turn_ws(g, (S + 0) % 2, O)
                        turn_y(O, g)
                    elif k == 8:
                        mix(g, O)

            def out_proj(n, off, S, ready, before, frees, split_start=0):
                pe.wait_ge(yl_ready, ready)
                for f in range(NF):
                    X = (1 - S) if f % 2 == 0 else S
                    if f == 1:
                        pe.wait_ge(*frees)
                    elif f >= 2:
                        pe.wait_ge(sum_out, before + (f - 1))
                    for k in range(OK):
                        tile(n, off + f * OK + k, X, yh[:, k, :], yl[:, k, :], k == 0, k == OK - 1)

            pe.wait_ge(v_out, NT * (VB - 1))
            for k in range(KC):
                in_tile(A0, k, k, 0)
                if k == 3:
                    pe.wait_ge(v_out, NT * VB)
                    turn_ws(0, 0, 1)
                elif k == 8:
                    mix(0, 1)
            with pe.Fori(0, G // 2 - 1) as j:
                n = j * APAIR + AL
                for e in range(2):
                    g, S, off = j * 2 + (e + 1), 1 - e, e * (KC + OT)
                    a_block(n, off, g, S)
                    pe.wait_ge(mix_ready, g + 1)
                    out_proj(n, off + KC, S, g, g * NF, (block_out, g + 1))
            g = G - 1
            a_block(AE, 0, g, 1)
            pe.wait_ge(mix_ready, g + 1)
            out_proj(AE, KC, 1, g, g * NF, (block_out, g + 1))
            pe.wait_ge(sum_out, g * NF + 3)
            turn_y(0, G)
            pe.wait_ge(sum_out, g * NF + 4)
            out_proj(AE, KC + OT, 0, G, G * NF, (yl_ready, G))

            S0 = NF * (G + 1)
            pe.wait_ge(sum_out, S0 - 1)
            for k in range(KC):
                if k < 4:
                    turn_x(k, KC) if k == 0 else turn_x(k, KC)
            pe.wait_ge(sum_out, S0)
            for k in range(KC):
                pe.wait_ge(xl_ready, KC + k + 1)
                in_tile(B0, k, k, 0)
                if k + 4 < KC:
                    turn_x(k + 4, KC)
            pe.wait_ge(xl_ready, 2 * KC)
            pe.wait_ge(wf_lo_ready, 1)
            for t in range(NT):
                o = ps[1][:, 0, t * H:(t + 1) * H]
                for k in range(KC):
                    a, b = xh[:, k, t * P:(t + 1) * P], xl[:, k, t * P:(t + 1) * P]
                    pe.matmul(o, a, wf_hi[:, k * H:(k + 1) * H], start=(k == 0), stop=False)
                    pe.matmul(o, a, wf_lo[:, k * H:(k + 1) * H], start=False, stop=False)
                    mm = pe.matmul(o, b, wf_hi[:, k * H:(k + 1) * H], start=False, stop=(k == KC - 1))
            mm.then_inc(f_psum, 1)
            pe.wait_ge(f_step, 5)
            for t in range(NT):
                mm = pe.transpose(ps[1][0:H, 1, t * P:(t + 1) * P], f_log[:, t, :], ident[:, :])
            mm.then_inc(fT_psum, 1)
            pe.wait_ge(cumT_ready, 1)
            for t in range(NT):
                mm = pe.transpose(ps[1][:, 2, t * H:(t + 1) * H], cum_T[0:H, t * P:(t + 1) * P],
                                  ident[0:H, 0:H])
            mm.then_inc(cumc_psum, 1)

            def head_steps(k, h, O):
                if k == 4:
                    pe.wait_ge(heads_out, h + 1)
                    pe.wait_ge(qk_normed, h + 1)
                    for s in range(2):
                        for t in range(NT):
                            mm = pe.transpose(ps[O][:, s, t * P:(t + 1) * P], qk[:, t, s, :], ident[:, :])
                        mm.then_inc(qkT_psum, 1)
                elif k == 6:
                    pe.wait_ge(qT_ready, h + 1)
                    pe.wait_ge(kT_ready, h + 1)
                    for i in range(NT):
                        pe.matmul(ps[O][:, i, 0:(i + 1) * P], qT[:, i * P:(i + 1) * P],
                                  kT[:, 0:(i + 1) * P], start=True, stop=False)
                        pe.matmul(ps[O][:, i, i * P:(i + 1) * P], ident_b[:, :], mask_b[:, :],
                                  start=False, stop=True).then_inc(scores, 1)
                elif k == 9:
                    pe.wait_ge(probs_ready, h * NT + NT)
                    b = 0
                    for i in range(NT):
                        for c in range(i + 1):
                            mm = pe.transpose(ps[O][:, b // 4, b % 4 * P:(b % 4 + 1) * P],
                                              probs[:, b * P:(b + 1) * P], ident[:, :])
                            b += 1
                    mm.then_inc(probsT_psum, 1)
                elif k == 12:
                    pe.wait_ge(probsT_act, h + 1)
                    pe.wait_ge(probsT_dve, h + 1)
                    for i in range(NT):
                        for c in range(i + 1):
                            b = row_at[i] + c * P
                            mm = pe.matmul(ps[O][:, 3, i * P:(i + 1) * P], probs_T[:, b:b + P],
                                           vn[:, c, :], start=(c == 0), stop=(c == i))
                    mm.then_inc(attended, 1)
                elif k == 14:
                    pe.wait_ge(yb_ready, h + 1)
                    for t in range(NT):
                        mm = pe.transpose(ps[O][:, 0, t * P:(t + 1) * P], yb[:, t, :], ident[:, :])
                    mm.then_inc(yT_psum, 1)

            def b_block(n, off, h, S):
                for k in range(KC):
                    in_tile(n, off + k, k, S)
                    head_steps(k, h - 1, 1 - S)

            pe.wait_ge(cumc_ready, 1)
            with pe.Fori(0, H // 2 - 1) as j:
                n = j * BPAIR + BL
                pe.wait_ge(sum_out, j * NF + (S0 - 1))
                for k in range(KC):
                    in_tile(n, k, k, 1)
                    if k == 3:
                        pe.wait_ge(sum_out, j * NF + S0)
                    head_steps(k, j * 2, 0)
                pe.wait_ge(yl_ready, j * 2 + (G + 1))
                b_block(n, KC, j * 2 + 2, 0)
                out_proj(n, 2 * KC, 0, j * 2 + (G + 2), j * NF + S0, (heads_out, j * 2 + 3))
            e = H // 2 - 1
            pe.wait_ge(sum_out, e * NF + S0 - 1)
            for k in range(KC):
                in_tile(BE, k, k, 1)
                if k == 3:
                    pe.wait_ge(sum_out, e * NF + S0)
                head_steps(k, H - 2, 0)
            pe.wait_ge(yl_ready, G + H - 1)
            for k in (4, 6, 9, 12, 14):
                head_steps(k, H - 1, 0)
            out_proj(BE, KC, 0, G + H, e * NF + S0, (yl_ready, G + H))

        @block.vector
        def _(dve):
            def split(n, i):
                s = i % R
                dve.wait_ge(hi_ready, n + (i + 1))
                dve.tensor_tensor(w_lo[:, s, :], w_raw[:, s, :], w_hi[:, s, :].bitcast(F32),
                                  ALU.subtract).then_inc(lo_ready, 1)

            def x_low(k, gain, done):
                dve.wait_ge(xh_ready, done + k + 1)
                dve.scalar_tensor_tensor(xl[:, k, :], ps[1][:, k % 4, :], gain[:, k:k + 1],
                                         xh[:, k, :].bitcast(F32), ALU.mult, ALU.subtract)\
                    .then_inc(xl_ready, 1)

            def x_stats(layer):
                dve.wait_ge(ssx_ready, (layer + 1) * NT)
                dve.tensor_scalar(msx[:, :], ssx[:, :], 1.0 / D, EPS, ALU.mult, ALU.add)\
                    .then_inc(msx_ready, 1)
                dve.wait_ge(rstd_ready, layer + 1)
                dve.tensor_scalar(hrstd[:, :], rstd[:, :], 0.5, None, ALU.mult).then_inc(hrstd_ready, 1)

            dve.wait_ge(rows_T, 1)
            dve.tensor_copy(cols[:, :], ps[0][:, 0, 0:2 * KC + G]).then_inc(cols_ready, 1)
            dve.wait_ge(cols_ready, 1)
            for k in range(4):
                x_low(k, a_gain, 0)
            for k in range(KC):
                split(0, k)
                if k + 4 < KC:
                    x_low(k + 4, a_gain, 0)
            x_stats(0)
            for k in range(KC):
                split(KC, k)
            with dve.Fori(1, VB // 2) as j:
                for k in range(2 * KC):
                    split(j * (2 * KC), k)

            def v_norm(g, s, count):
                dve.wait_ge(vg_loaded[s], count)
                for c in range(NT):
                    a = v[:, ds(g, 1), c, :].rearrange("p g d -> p (g d)")
                    ins = dve.scalar_tensor_tensor(a, a, vrstd[:, c:c + 1], vg_row[:, s, :],
                                                   ALU.mult, ALU.mult)
                ins.then_inc(v_normed, 1)

            def ws_leave(g, O):
                dve.wait_ge(ws_T_psum, g + 1)
                dve.tensor_copy(ws_T[:, :], ps[O][:, 3, 0:P]).then_inc(ws_T_ready, 1)

            def mix_leave(g, O):
                dve.wait_ge(mixed, g + 1)
                dve.tensor_scalar(v[:, ds(g, 1), :, :].rearrange("p g c d -> p (g c d)"),
                                  ps[O][:, 2:4, :].rearrange("p b c -> p (b c)"),
                                  b_s_cols[:, ds(g, 1)], None, ALU.add).then_inc(mix_ready, 1)

            def y_low(O, count):
                dve.wait_ge(yh_ready, count)
                dve.tensor_tensor(yl[:, :, :], ps[O][:, 0:OK, :], yh[:, :, :].bitcast(F32),
                                  ALU.subtract).then_inc(yl_ready, 1)

            def leave(g, S):
                dve.wait_ge(u_ready, g + 1)
                dve.wait_ge(mix_ready, g + 1)
                dve.tensor_tensor(ug[:, :, :], ug[:, :, :],
                                  v[:, ds(g, 1), :, :].rearrange("p g c d -> p (g c) d"), ALU.mult)\
                    .then_inc(gate_step, 1)
                dve.wait_ge(tanh_ready, g + 1)
                dve.scalar_tensor_tensor(zz[:, :, :], zz[:, :, :], 1.0, ps[S][:, :, GD:2 * GD],
                                         ALU.add, ALU.mult).then_inc(block_out, 1)
                dve.wait_ge(gate_step, g + 1)
                dve.wait_ge(block_out, g + 1)
                for t in range(NT):
                    ins = dve.scalar_tensor_tensor(ug[:, t, :], ug[:, t, :], hrstd[:, t:t + 1], zz[:, t, :],
                                                   ALU.mult, ALU.mult)
                ins.then_inc(y_ready, 1)

            def a_block(n, off, g, S):
                for k in range(KC):
                    split(n, off + k)
                    if k == 3:
                        v_norm(g, (S + 0) % 2, g_count[0])
                    elif k == 5:
                        ws_leave(g, 1 - S)
                    elif k == 6:
                        y_low(1 - S, g)
                    elif k == 10:
                        mix_leave(g, 1 - S)

            g_count = [0]

            def add_out(n, i, f, S):
                dve.wait_ge(tile_used, n + i)
                for b in range(2):
                    o = acc[:, 2 * b:2 * b + 2, f * FB:(f + 1) * FB]
                    ins = dve.tensor_tensor(o, ps[S][:, 2 * b:2 * b + 2, :], o, ALU.add)
                ins.then_inc(sum_out, 1)

            def out_sets(S):
                return [1 - S, S, 1 - S, S]

            for k in range(KC):
                split(A0, k)
                if k == 2:
                    dve.wait_ge(vsq_ready, NT * VB)
                    dve.tensor_reduce(vms[:, 0, :], vsq[:, :, :], AX.X, ALU.add).then_inc(vms_ready, 1)
                    dve.wait_ge(vms_ready, 1)
                    dve.tensor_scalar(vms[:, 1, :], vms[:, 0, :], 1.0 / AW, EPS, ALU.mult, ALU.add)\
                        .then_inc(vms_ready, 1)
                elif k == 4:
                    ws_leave(0, 1)
                elif k == 5:
                    dve.wait_ge(vrstd_ready, 1)
                    v_norm(0, 0, 16)
                elif k == 10:
                    dve.wait_ge(v_out, NT * VB)
                    dve.tensor_copy(vms[:, 0, :], vrstd[:, :]).then_inc(sum_out, NF)
                    mix_leave(0, 1)
            leave(0, 0)

            def a_tail(n, off, count, S):
                sets = out_sets(S)
                for i in range(OT):
                    split(n, off + i)
                    if i == 2:
                        leave(count, S)
                    elif i >= 4 and i % 2 == 0:
                        f = (i - 4) // 2
                        add_out(n, off + OK * (f + 1), f, sets[f])

            def rest(n, off, i, S):
                sets = out_sets(S)
                if i == 0:
                    add_out(n, off - OK, 2, sets[2])
                elif i == 2:
                    add_out(n, off, 3, sets[3])

            def a_block_after(n, off, g, S, prev_S):
                for k in range(KC):
                    split(n, off + k)
                    if prev_S is not None:
                        rest(n, off, k, prev_S)
                    if k == 3:
                        v_norm(g, 1 if S == 1 else 0, g_count[0])
                    elif k == 5:
                        ws_leave(g, 1 - S)
                    elif k == 6:
                        y_low(1 - S, g)
                    elif k == 10:
                        mix_leave(g, 1 - S)

            def pair(n, j, first):
                g_count[0] = j * 16 + 16
                a_block_after(n, 0, j * 2 + 1, 1, None if first else 0)
                a_tail(n, KC, j * 2 + 1, 1)
                g_count[0] = j * 16 + 32
                a_block_after(n, KC + OT, j * 2 + 2, 0, 1)
                a_tail(n, 2 * KC + OT, j * 2 + 2, 0)

            pair(AL, 0, True)
            with dve.Fori(1, G // 2 - 1) as j:
                pair(j * APAIR + AL, j, False)
            g_count[0] = 16 * (G // 2)
            a_block_after(AE, 0, G - 1, 1, 0)
            a_tail(AE, KC, G - 1, 1)
            add_out(AE, KC + OT - OK, 2, 0)
            add_out(AE, KC + OT, 3, 1)
            y_low(0, G)
            for i in range(OT):
                split(AE, KC + OT + i)
                if i % 2 == 0 and i >= 2:
                    f = i // 2 - 1
                    add_out(AE, KC + OT + OK * (f + 1), f, out_sets(0)[f])
            add_out(AE, KC + 2 * OT, 3, 0)

            for k in range(4):
                x_low(k, b_gain, KC)
            for k in range(KC):
                split(B0, k)
                if k + 4 < KC:
                    x_low(k + 4, b_gain, KC)
            dve.wait_ge(wf_hi_ready, 1)
            dve.tensor_tensor(wf_lo, wf_raw, wf_hi.bitcast(F32), ALU.subtract).then_inc(wf_lo_ready, 1)
            dve.wait_ge(y_ready, G)
            x_stats(1)
            dve.wait_ge(gains_loaded, 48)
            dve.tensor_scalar(qg_row, qg_row, SCALE, None, ALU.mult).then_inc(gains_ready, 1)
            dve.wait_ge(f_psum, 1)
            for t in range(NT):
                ins = dve.scalar_tensor_tensor(f_log[:, t, :], ps[1][:, 0, t * H:(t + 1) * H],
                                               rstd[:, t:t + 1], fb_row, ALU.mult, ALU.add)
            ins.then_inc(f_step, 1)
            dve.wait_ge(f_step, 1)
            dve.tensor_scalar(f_e[:, :, :], f_log[:, :, :], -1.0, None, ALU.mult).then_inc(f_step, 1)
            dve.wait_ge(f_step, 2)
            dve.tensor_tensor(f_abs[:, :, :], f_log[:, :, :], f_e[:, :, :], ALU.max).then_inc(f_step, 1)
            dve.wait_ge(f_act, 2)
            dve.tensor_scalar(f_e[:, :, :], f_log[:, :, :], 0.0, None, ALU.min).then_inc(f_step, 1)
            dve.wait_ge(f_step, 4)
            dve.tensor_tensor(f_log[:, :, :], f_e[:, :, :], f_abs[:, :, :], ALU.subtract).then_inc(f_step, 1)
            dve.wait_ge(fT_psum, 1)
            dve.tensor_copy(f_T[0:H, :], ps[1][0:H, 1, :]).then_inc(f_step, 1)
            dve.wait_ge(f_step, 6)
            dve.wait_ge(const_ready, 8)
            dve.tensor_tensor_scan(cum_T[0:H, :], f_one[0:H, :], f_T[0:H, :], 0.0, ALU.mult, ALU.add)\
                .then_inc(cumT_ready, 1)
            dve.wait_ge(cumc_psum, 1)
            dve.tensor_copy(cum_col[:, :, :], ps[1][:, 2, 0:NT * H].rearrange("p (t h) -> p t h", t=NT))\
                .then_inc(cumc_ready, 1)
            dve.wait_ge(cumc_ready, 1)
            dve.wait_ge(gains_ready, 1)

            def head_leave(n, i, h, S):
                dve.wait_ge(tile_used, n + i)
                dve.wait_ge(tanh_b, h + 1)
                dve.wait_ge(v_b, h + 1)
                dve.tensor_copy(qk[:, :, :, :].rearrange("p t s d -> p t (s d)"),
                                ps[S][:, :, 0:2 * HD]).then_inc(qk_out, 1)
                dve.scalar_tensor_tensor(zb[:, :, :], zb[:, :, :], 1.0, ps[S][:, :, 3 * HD:4 * HD],
                                         ALU.add, ALU.mult).then_inc(heads_out, 1)

            def head_norm(h):
                dve.wait_ge(qkss_ready, h + 1)
                dve.tensor_scalar(qkms[:, :, :], qkss[:, :, :], 1.0 / HD, EPS, ALU.mult, ALU.add)\
                    .then_inc(qkms_ready, 1)
                dve.wait_ge(qkr_ready, h + 1)
                for s in range(2):
                    ins = dve.tensor_tensor(qkr[:, :, s], qkr[:, :, s], rstd[:, :], ALU.mult)
                ins.then_inc(qkr_scaled, 1)
                dve.wait_ge(qkr_scaled, h + 1)
                for t in range(NT):
                    for s, g in ((0, qg_row), (1, kg_row)):
                        ins = dve.scalar_tensor_tensor(qk[:, t, s, :], qk[:, t, s, :], qkr[:, t, s:s + 1], g,
                                                       ALU.mult, ALU.mult)
                ins.then_inc(qk_normed, 1)

            def row_logits(h, i, O, s):
                dve.wait_ge(scores, h * NT + (i + 1))
                p = probs[:, row_at[i]:row_at[i + 1]]
                dve.scalar_tensor_tensor(p, ps[O][:, i, 0:(i + 1) * P],
                                         cum_col[:, i, ds(h, 1)], cum_row[:, s, 0:(i + 1) * P],
                                         ALU.add, ALU.subtract).then_inc(logits, 1)
                dve.wait_ge(logits, h * NT + (i + 1))
                dve.tensor_reduce(nmax[:, i:i + 1], p, AX.X, ALU.max, negate=True).then_inc(nmax_ready, 1)

            def head_steps(k, h, O, s, count, hh):
                if k == 5:
                    dve.wait_ge(qkT_psum, h * 2 + 2)
                    dve.tensor_copy(kT, ps[O][:, 1, :]).then_inc(kT_ready, 1)
                elif k == 7:
                    dve.wait_ge(cum_loaded[s], count)
                    row_logits(h, 0, O, s)
                    row_logits(h, 1, O, s)
                elif k == 8:
                    row_logits(h, 2, O, s)
                    row_logits(h, 3, O, s)
                elif k == 11:
                    dve.wait_ge(probsT_psum, h + 1)
                    dve.tensor_copy(probs_T[:, 8 * P:NB * P], ps[O][:, 2, 0:(NB - 8) * P])\
                        .then_inc(probsT_dve, 1)
                    dve.wait_ge(probs_ready, h * NT + NT)
                    dve.reciprocal(rsum[:, :], rsum[:, :]).then_inc(rinv_ready, 1)
                    dve.wait_ge(rinv_ready, h * 2 + 1)
                    dve.tensor_tensor(rinv[:, :], rsum[:, :], hrstd[:, :], ALU.mult).then_inc(rinv_ready, 1)
                elif k == 13:
                    dve.wait_ge(attended, h + 1)
                    dve.wait_ge(rinv_ready, h * 2 + 2)
                    for i in range(NT):
                        ins = dve.scalar_tensor_tensor(yb[:, i, :], ps[O][:, 3, i * P:(i + 1) * P],
                                                       rinv[:, i:i + 1], zb[:, i, :], ALU.mult, ALU.mult)
                    ins.then_inc(yb_ready, 1)
                elif k == 15:
                    dve.wait_ge(yh_ready, h + (G + 1))
                    dve.tensor_tensor(yl[:, hh, :], ps[O][:, 0, :], yh[:, hh, :].bitcast(F32),
                                      ALU.subtract).then_inc(yl_ready, 1)

            def b_pair(n, j, first):
                for k in range(KC):
                    split(n, k)
                    if not first:
                        rest(n, 0, k, 0)
                    head_steps(k, j * 2, 0, 0, j * 16 + 16, 0)
                for k in range(KC):
                    split(n, KC + k)
                    if k == 2:
                        head_leave(n, KC, j * 2 + 1, 1)
                    elif k == 3:
                        head_norm(j * 2 + 1)
                    head_steps(k, j * 2 + 1, 1, 1, j * 16 + 16, 1)
                for i in range(OT):
                    split(n, 2 * KC + i)
                    if i == 2:
                        head_leave(n, 2 * KC, j * 2 + 2, 0)
                    elif i == 3:
                        head_norm(j * 2 + 2)
                    elif i >= 4 and i % 2 == 0:
                        f = (i - 4) // 2
                        add_out(n, 2 * KC + OK * (f + 1), f, out_sets(0)[f])

            head_leave(B0, KC, 0, 0)
            head_norm(0)
            b_pair(BL, 0, True)
            with dve.Fori(1, H // 2 - 1) as j:
                b_pair(j * BPAIR + BL, j, False)
            for k in range(KC):
                split(BE, k)
                rest(BE, 0, k, 0)
                head_steps(k, H - 2, 0, 0, 16 * (H // 2), 0)
            for i in range(3):
                split(BE, KC + i)
            head_leave(BE, KC, H - 1, 1)
            head_norm(H - 1)
            for k in (5, 7, 8, 11, 13, 15):
                head_steps(k, H - 1, 0, 1, 16 * (H // 2), 1)
            for i in range(3, OT):
                split(BE, KC + i)
                if i in (4, 6):
                    add_out(BE, KC + i - 2, (i - 4) // 2, out_sets(0)[(i - 4) // 2])
            for f in (2, 3):
                add_out(BE, KC + OK * (f + 1), f, out_sets(0)[f])


_INS = ["x", "a_norm_g", "a_w_in", "a_v_norm_g", "a_w_s", "a_b_s", "a_w_out",
        "b_norm_g", "b_w_in", "b_f_bias", "b_q_norm_g", "b_k_norm_g", "b_w_out"]


def kernel(**inputs):
    import numpy as _np
    import concourse.bacc as _bacc
    from concourse import mybir as _mybir
    from concourse.bass_utils import run_bass_kernel_spmd as _run

    nc = _bacc.Bacc("TRN2", target_bir_lowering=False, num_devices=1)
    arrays, args = {}, []
    for name in _INS:
        a = _np.ascontiguousarray(inputs[name])
        arrays[f"in_{name}_dram"] = a
        args.append(nc.dram_tensor(f"in_{name}_dram", a.shape, _mybir.dt.from_np(a.dtype),
                                   kind="ExternalInput").ap())
    out = nc.dram_tensor("out_dram", inputs["x"].shape, _mybir.dt.float32, kind="ExternalOutput").ap()
    build_trunk(nc, *args, out)
    r = _run(nc, [arrays], core_ids=[0])
    return r.results[0]["out_dram"]
```

```python
from contextlib import ExitStack

import concourse.bass as bass
from concourse import mybir

F32 = mybir.dt.float32
F32R = mybir.dt.float32r
BF16 = mybir.dt.bfloat16
ACT = mybir.ActivationFunctionType
ALU = mybir.AluOpType
AX = mybir.AxisListType
ds = bass.ds

P = 128
EPS = 1e-6


def build_trunk(nc, x, a_norm_g, a_w_in, a_v_norm_g, a_w_s, a_b_s, a_w_out,
                b_norm_g, b_w_in, b_f_bias, b_q_norm_g, b_k_norm_g, b_w_out, out):
    SEQ, D = x.shape[1], x.shape[2]
    NT = SEQ // P
    KC = D // P
    AW = a_w_out.shape[1]
    G = a_w_s.shape[1]
    GD = AW // G
    H = b_f_bias.shape[1]
    HD = b_q_norm_g.shape[1]
    FB = 512
    NF = D // FB
    VB = AW // FB
    R = 4
    LEAD = R - 1
    OK = GD // P
    assert (NT, NF, GD, HD, OK, SEQ) == (4, 4, 256, P, 2, 512) and G == H == 16 == KC
    OT = NF * OK
    SCALE = float(HD) ** -0.5
    NEG = -1e30

    A0 = VB * KC
    AL = A0 + KC
    APAIR = 2 * (KC + OT)
    AE = AL + (G // 2 - 1) * APAIR
    B0 = AE + KC + 2 * OT
    BL = B0 + KC
    BPAIR = 2 * KC + OT
    BE = BL + (H // 2 - 2) * BPAIR
    TILES = BE + 3 * KC + 2 * OT
    assert A0 % R == AL % R == APAIR % R == AE % R == B0 % R == BPAIR % R == 0

    x_t = x[0].rearrange("(t p) d -> p t d", p=P)
    out_t = out[0].rearrange("(t p) d -> p t d", p=P)
    a_in = a_w_in[0]
    a_uz = a_w_in[0].rearrange("r (s c) -> r s c", s=3)[:, 0:3:2, :]
    a_out = a_w_out[0]
    b_qkvz = b_w_in[0][:, 0:4 * D].rearrange("r (s c) -> r s c", s=4)
    b_f = b_w_in[0][:, 4 * D:4 * D + H].rearrange("(k p) h -> p k h", p=P)
    b_out = b_w_out[0]
    cum_dram = nc.dram_tensor("cum_rows", [H, SEQ], F32).ap()

    with ExitStack() as ctx:
        def sb(name, shape, dt=F32):
            return ctx.enter_context(nc.sbuf_tensor(name, shape, dt))

        def sem(name):
            return ctx.enter_context(nc.semaphore(name))

        acc = sb("acc", [P, NT, D])
        xh = sb("xh", [P, KC, SEQ], F32R)
        xl = sb("xl", [P, KC, SEQ], F32R)
        v_all = sb("v_all", [P, G * NT * GD])
        v = v_all[:, :].rearrange("p (g c d) -> p g c d", g=G, c=NT)
        yh = sb("yh", [P, OK, SEQ], F32R)
        yl = sb("yl", [P, OK, SEQ], F32R)
        ug = sb("ug", [P, NT, GD])
        zz = sb("zz", [P, NT, GD])
        w_raw = sb("w_raw", [P, R, FB])
        w_hi = sb("w_hi", [P, R, FB], F32R)
        w_lo = sb("w_lo", [P, R, FB], F32R)
        ident = sb("ident", [P, P])
        ident_b = sb("ident_b", [P, P], BF16)
        mask_b = sb("mask_b", [P, P], BF16)
        ws_raw = sb("ws_raw", [P, 2, P])
        ws_T = sb("ws_T", [P, P])
        vg_row = sb("vg_row", [P, 2, GD])
        rows = sb("rows", [2 * KC + G, P])
        cols = sb("cols", [P, 2 * KC + G])
        mhalf = sb("mhalf", [P, 2 * NT])
        ssx = sb("ssx", [P, NT])
        msx = sb("msx", [P, NT])
        rstd = sb("rstd", [P, NT])
        hrstd = sb("hrstd", [P, NT])
        vsq = sb("vsq", [P, NT, VB])
        vms = sb("vms", [P, 2, NT])
        vrstd = sb("vrstd", [P, NT])
        qkss = sb("qkss", [P, NT, 2])
        qkms = sb("qkms", [P, NT, 2])
        qkr = sb("qkr", [P, NT, 2])
        nmax = sb("nmax", [P, NT])
        rsum = sb("rsum", [P, NT])
        rinv = sb("rinv", [P, NT])

        a_gain, b_gain, b_s_cols = cols[:, 0:KC], cols[:, KC:2 * KC], cols[:, 2 * KC:]

        at = [0]

        def part(n, pattern=None, **sizes):
            ap = v_all[:, at[0]:at[0] + n]
            at[0] += n
            return ap.rearrange(pattern, **sizes) if pattern else ap

        qk = part(NT * 2 * HD, "p (t s d) -> p t s d", t=NT, s=2)
        vn = part(NT * HD, "p (t d) -> p t d", t=NT)
        zb = part(NT * HD, "p (t d) -> p t d", t=NT)
        yb = part(NT * HD, "p (t d) -> p t d", t=NT)
        qT = part(SEQ)
        kT = part(SEQ)
        NB = NT * (NT + 1) // 2
        probs = part(NB * P)
        probs_T = part(NB * P)
        cum_row = part(2 * SEQ, "p (b s) -> p b s", b=2)
        qg_row = part(HD)
        kg_row = part(HD)
        fb_col = part(1)
        wf_raw = part(KC * H)
        rstd_row, f_lin, f_abs, f_min, f_log, f_one, cum_T = (part(SEQ)[0:H, :] for _ in range(7))
        cum_col = part(NT * H, "p (t h) -> p t h", t=NT)
        junk = part(D)
        row_at = [i * (i + 1) // 2 * P for i in range(NT + 1)]
        wf_hi, wf_lo = yh[:, 0, 0:KC * H], yl[:, 0, 0:KC * H]

        ps = [ctx.enter_context(nc.psum_tensor(f"ps{i}", [P, 4, 512], F32)) for i in range(2)]

        w_loaded = [sem(f"w_loaded{s}") for s in range(R)]
        hi_ready = sem("hi_ready")
        lo_ready = sem("lo_ready")
        tile_used = sem("tile_used")
        x_loaded = [sem(f"x_loaded{c}") for c in range(NF)]
        rows_loaded = sem("rows_loaded")
        const_ready = sem("const_ready")
        rows_T = sem("rows_T")
        cols_ready = sem("cols_ready")
        xT_ready = sem("xT_ready")
        xh_ready = sem("xh_ready")
        xl_ready = sem("xl_ready")
        ssx_ready = sem("ssx_ready")
        msx_ready = sem("msx_ready")
        rstd_ready = sem("rstd_ready")
        hrstd_ready = sem("hrstd_ready")
        v_out = sem("v_out")
        vsq_ready = sem("vsq_ready")
        vms_ready = sem("vms_ready")
        vrstd_ready = sem("vrstd_ready")
        ws_loaded = [sem("ws_loaded0"), sem("ws_loaded1")]
        vg_loaded = [sem("vg_loaded0"), sem("vg_loaded1")]
        mask_turn = sem("mask_turn")
        ws_masked = sem("ws_masked")
        ws_T_psum = sem("ws_T_psum")
        ws_T_ready = sem("ws_T_ready")
        v_normed = sem("v_normed")
        mixed = sem("mixed")
        mix_ready = sem("mix_ready")
        u_ready = sem("u_ready")
        tanh_ready = sem("tanh_ready")
        block_out = sem("block_out")
        gate_step = sem("gate_step")
        y_ready = sem("y_ready")
        yT_psum = sem("yT_psum")
        yh_ready = sem("yh_ready")
        yl_ready = sem("yl_ready")
        sum_out = sem("sum_out")
        heads_out = sem("heads_out")
        qk_out = sem("qk_out")
        tanh_b = sem("tanh_b")
        v_b = sem("v_b")
        qkss_ready = sem("qkss_ready")
        qkms_ready = sem("qkms_ready")
        qkr_ready = sem("qkr_ready")
        qkr_scaled = sem("qkr_scaled")
        qk_normed = sem("qk_normed")
        qkT_psum = sem("qkT_psum")
        qT_ready = sem("qT_ready")
        kT_ready = sem("kT_ready")
        scores = sem("scores")
        logits = sem("logits")
        nmax_ready = sem("nmax_ready")
        probs_ready = sem("probs_ready")
        rinv_ready = sem("rinv_ready")
        probsT_psum = sem("probsT_psum")
        probsT_act = sem("probsT_act")
        probsT_dve = sem("probsT_dve")
        attended = sem("attended")
        yb_ready = sem("yb_ready")
        gains_loaded = sem("gains_loaded")
        gains_ready = sem("gains_ready")
        wf_loaded = sem("wf_loaded")
        wf_hi_ready = sem("wf_hi_ready")
        wf_lo_ready = sem("wf_lo_ready")
        f_psum = sem("f_psum")
        f_step = sem("f_step")
        f_act = sem("f_act")
        rstdT_psum = sem("rstdT_psum")
        cumT_ready = sem("cumT_ready")
        cum_stored = sem("cum_stored")
        cumc_psum = sem("cumc_psum")
        cumc_ready = sem("cumc_ready")
        cum_loaded = [sem("cum_loaded0"), sem("cum_loaded1")]
        out_stored = sem("out_stored")

        block = ctx.enter_context(nc.Block())

        @block.sync
        def _(sp):
            def load(n, i, src, first=False):
                s = i % R
                if not first:
                    sp.wait_ge(lo_ready, n + (i - R + 1))
                dst = w_raw[:, s, :]
                if len(src.shape) == 3:
                    dst = dst.rearrange("p (s c) -> p s c", s=src.shape[1])
                sp.dma_start(dst, src).then_inc(w_loaded[s], 16)

            def v_block(n, b, first=False):
                for k in range(KC):
                    load(n, k, a_in[k * P:(k + 1) * P, ds(AW + b * FB, FB)], first and k < R)

            def a_block(n, off, g):
                for k in range(KC):
                    load(n, off + k, a_uz[k * P:(k + 1) * P, :, ds(g * GD, GD)])

            def out_proj(n, off, w, row):
                for f in range(NF):
                    for k in range(OK):
                        load(n, off + f * OK + k, w[ds(row + k * P, P), f * FB:(f + 1) * FB])

            def b_block(n, off, h):
                for k in range(KC):
                    load(n, off + k, b_qkvz[k * P:(k + 1) * P, :, ds(h * HD, HD)])

            v_block(0, 0, first=True)
            v_block(KC, 1)
            with sp.Fori(1, VB // 2) as j:
                v_block(j * (2 * KC), j * 2)
                v_block(j * (2 * KC) + KC, j * 2 + 1)
            a_block(A0, 0, 0)
            with sp.Fori(0, G // 2 - 1) as j:
                n = j * APAIR + AL
                a_block(n, 0, j * 2 + 1)
                out_proj(n, KC, a_out, j * (2 * GD))
                a_block(n, KC + OT, j * 2 + 2)
                out_proj(n, 2 * KC + OT, a_out, j * (2 * GD) + GD)
            a_block(AE, 0, G - 1)
            out_proj(AE, KC, a_out, (G - 2) * GD)
            out_proj(AE, KC + OT, a_out, (G - 1) * GD)
            b_block(B0, 0, 0)
            with sp.Fori(0, H // 2 - 2) as j:
                n = j * BPAIR + BL
                b_block(n, 0, j * 2 + 1)
                b_block(n, KC, j * 2 + 2)
                out_proj(n, 2 * KC, b_out, j * (2 * HD))
            for e in range(3):
                b_block(BE, e * KC, H - 3 + e)
            for e in range(2):
                out_proj(BE, 3 * KC + e * OT, b_out, (H - 4 + 2 * e) * HD)
            for f in range(NF):
                sp.wait_ge(sum_out, NF * (1 + G + H // 2 - 1) + f + 1)
                sp.dma_start(out_t[:, :, f * FB:(f + 1) * FB],
                             acc[:, :, f * FB:(f + 1) * FB]).then_inc(out_stored, 16)
            sp.wait_ge(out_stored, 16 * NF)

        @block.gpsimd
        def _(pool):
            pool.memset(ident[:, :], 0.0).then_inc(const_ready, 1)
            pool.memset(ident_b[:, :], 0.0).then_inc(const_ready, 1)
            pool.memset(mask_b[:, :], 0.0).then_inc(const_ready, 1)
            pool.memset(mhalf[:, :], -0.5).then_inc(const_ready, 1)
            pool.wait_ge(const_ready, 4)
            for m in (ident, ident_b):
                pool.affine_select(out=m[:, :], in_=m[:, :], compare_op=ALU.not_equal, fill=1.0,
                                   base=0, pattern=[[-1, P]], channel_multiplier=1).then_inc(const_ready, 1)
            pool.affine_select(out=mask_b[:, :], in_=mask_b[:, :], compare_op=ALU.is_ge, fill=NEG,
                               base=0, pattern=[[-1, P]], channel_multiplier=1).then_inc(const_ready, 1)

            def power(dst, src, n):
                return pool.tensor_tensor(dst, src, mhalf[:, 0:n], ALU.pow)

            pool.wait_ge(msx_ready, 1)
            power(rstd[:, :], msx[:, :], NT).then_inc(rstd_ready, 1)

            def load_group(g, s, first=False):
                if not first:
                    pool.wait_ge(ws_T_psum, g - 1)
                    pool.wait_ge(v_normed, g - 1)
                pool.dma_start(ws_raw[:, s, :], a_w_s[0, ds(g, 1)].rearrange("a t s -> t (a s)"))\
                    .then_inc(ws_loaded[s], 16)
                pool.dma_start(vg_row[:, s, :], a_v_norm_g[0:1, ds(g * GD, GD)].broadcast_to([P, GD]))\
                    .then_inc(vg_loaded[s], 16)

            def mask_group(g, s, count):
                pool.wait_ge(ws_loaded[s], count)
                pool.sem_inc(mask_turn, 1)
                pool.affine_select(out=ws_raw[:, s, :], in_=ws_raw[:, s, :], compare_op=ALU.is_ge,
                                   fill=0.0, base=0, pattern=[[-1, P]], channel_multiplier=1)\
                    .then_inc(ws_masked, 1)

            load_group(0, 0, first=True)
            load_group(1, 1, first=True)
            mask_group(0, 0, 16)
            pool.wait_ge(vms_ready, 2)
            power(vrstd[:, :], vms[:, 1, :], NT).then_inc(vrstd_ready, 1)
            mask_group(1, 1, 16)
            with pool.Fori(1, G // 2) as j:
                for s in range(2):
                    load_group(j * 2 + s, s)
                    mask_group(j * 2 + s, s, j * 16 + 16)

            pool.wait_ge(y_ready, G)
            pool.dma_start(qg_row, b_q_norm_g[0:1, :].broadcast_to([P, HD])).then_inc(gains_loaded, 16)
            pool.dma_start(kg_row, b_k_norm_g[0:1, :].broadcast_to([P, HD])).then_inc(gains_loaded, 16)
            pool.dma_start(fb_col[0:H, :], b_f_bias.rearrange("a h -> h a")).then_inc(gains_loaded, 16)
            pool.dma_start(wf_raw.rearrange("p (k h) -> p k h", h=H), b_f).then_inc(wf_loaded, 16)
            pool.memset(f_one, 1.0).then_inc(const_ready, 1)
            pool.wait_ge(msx_ready, 2)
            pool.wait_ge(hrstd_ready, 1)
            power(rstd[:, :], msx[:, :], NT).then_inc(rstd_ready, 1)
            pool.wait_ge(cumT_ready, 1)
            pool.dma_start(cum_dram, cum_T).then_inc(cum_stored, 16)
            pool.wait_ge(cum_stored, 16)

            def load_cum(h, s, first=False):
                if not first:
                    pool.wait_ge(logits, (h - 1) * NT)
                pool.dma_start(cum_row[:, s, :], cum_dram[ds(h, 1), :].broadcast_to([P, SEQ]))\
                    .then_inc(cum_loaded[s], 16)

            def head_power(h):
                pool.wait_ge(qkms_ready, h + 1)
                power(qkr[:, :, :], qkms[:, :, :], 2 * NT).then_inc(qkr_ready, 1)

            load_cum(0, 0, first=True)
            load_cum(1, 1, first=True)
            head_power(0)
            head_power(1)
            with pool.Fori(1, H // 2) as j:
                for s in range(2):
                    load_cum(j * 2 + s, s)
                    head_power(j * 2 + s)

        @block.scalar
        def _(act):
            for r, src in ((0, a_norm_g[0].rearrange("(k p) -> k p", p=P)),
                           (KC, b_norm_g[0].rearrange("(k p) -> k p", p=P)), (2 * KC, a_b_s[0])):
                act.dma_start(rows[r:r + src.shape[0], :], src).then_inc(rows_loaded, 16)
            for c in range(NF):
                act.dma_start(acc[:, :, c * FB:(c + 1) * FB],
                              x_t[:, :, c * FB:(c + 1) * FB]).then_inc(x_loaded[c], 16)

            def split(n, q, i, first=False):
                s = i % R
                act.wait_ge(w_loaded[s], q * 16 + (i // R * 16 + 16))
                if not first:
                    act.wait_ge(tile_used, n + (i - R + 1))
                act.activation(w_hi[:, s, :], w_raw[:, s, :], ACT.Copy).then_inc(hi_ready, 1)

            def step(n, q, i):
                split(n, q, i + LEAD)

            def x_high(k, gain, done):
                act.wait_ge(xT_ready, done + k + 1)
                act.activation(xh[:, k, :], ps[1][:, k % 4, :], ACT.Copy,
                               scale=gain[:, k:k + 1]).then_inc(xh_ready, 1)

            def x_square(t, done):
                act.activation(junk, acc[:, t, :], ACT.Square, accum_out=ssx[:, t:t + 1])\
                    .then_inc(ssx_ready, 1)
                act.wait_ge(ssx_ready, done + t + 1)

            act.wait_ge(cols_ready, 1)
            for k in range(4):
                x_high(k, a_gain, 0)
                if k < LEAD:
                    split(0, 0, k, first=True)
            for k in range(KC):
                if k + 4 < KC:
                    x_high(k + 4, a_gain, 0)
                split(0, 0, k + LEAD, first=k + LEAD < R)
                if k in (12, 13, 14, 15):
                    act.wait_ge(x_loaded[NF - 1], 16)
                    x_square(k - 12, 0)

            def v_leave(n, i, S, b):
                act.wait_ge(tile_used, n + i)
                for t in range(NT):
                    act.activation(v[:, ds(b * 2, 2), t, :], ps[S][:, t, :].rearrange("p (g d) -> p g d", g=2),
                                   ACT.Gelu_apprx_tanh, scale=rstd[:, t:t + 1]).then_inc(v_out, 1)
                act.wait_ge(vsq_ready, b * NT)
                for t in range(NT):
                    act.wait_ge(v_out, b * NT + (t + 1))
                    act.activation((ug, zz)[t // 2][:, t % 2 * 2:t % 2 * 2 + 2, :], v[:, ds(b * 2, 2), t, :],
                                   ACT.Square, accum_out=vsq[:, t, ds(b, 1)]).then_inc(vsq_ready, 1)

            act.wait_ge(rstd_ready, 1)
            v_leave(0, KC, 0, 0)
            for k in range(KC):
                step(KC, KC // R, k)
            v_leave(KC, KC, 1, 1)
            with act.Fori(1, VB // 2) as j:
                for e in range(2):
                    n, q = j * (2 * KC), j * (2 * KC // R)
                    for k in range(KC):
                        step(n, q, e * KC + k)
                    v_leave(n, (e + 1) * KC, e, j * 2 + e)

            act.wait_ge(hrstd_ready, 1)

            def leave(n, i, g, S):
                act.wait_ge(tile_used, n + i)
                act.wait_ge(y_ready, g)
                act.wait_ge(yT_psum, g)
                for t in range(NT):
                    ins = act.activation(ug[:, t, :], ps[S][:, t, 0:GD], ACT.Gelu_apprx_tanh,
                                         scale=rstd[:, t:t + 1])
                ins.then_inc(u_ready, 1)
                for t in range(NT):
                    ins = act.activation(zz[:, t, :], ps[S][:, t, GD:2 * GD], ACT.Tanh,
                                         scale=hrstd[:, t:t + 1])
                ins.then_inc(tanh_ready, 1)

            def y_high(O, count):
                act.wait_ge(yT_psum, count)
                act.activation(yh[:, :, :], ps[O][:, 0:OK, :], ACT.Copy).then_inc(yh_ready, 1)

            def a_block(n, q, off, g, S):
                for k in range(KC):
                    step(n, q, off + k)
                    if k == 2:
                        y_high(1 - S, g)
                leave(n, off + KC, g, S)

            def out_steps(n, q, off):
                for i in range(OT):
                    step(n, q, off + i)

            for k in range(KC):
                step(A0, A0 // R, k)
            leave(A0, KC, 0, 0)
            with act.Fori(0, G // 2 - 1) as j:
                n, q = j * APAIR + AL, j * (APAIR // R) + AL // R
                a_block(n, q, 0, j * 2 + 1, 1)
                out_steps(n, q, KC)
                a_block(n, q, KC + OT, j * 2 + 2, 0)
                out_steps(n, q, 2 * KC + OT)
            a_block(AE, AE // R, 0, G - 1, 1)
            out_steps(AE, AE // R, KC)
            y_high(0, G)
            out_steps(AE, AE // R, KC + OT)

            for k in range(4):
                x_high(k, b_gain, KC)
            act.wait_ge(y_ready, G)
            for k in range(KC):
                if k + 4 < KC:
                    x_high(k + 4, b_gain, KC)
                step(B0, B0 // R, k)
                if k in (3, 5, 7, 9):
                    x_square((k - 3) // 2, NT)
                elif k == 10:
                    act.wait_ge(wf_loaded, 16)
                    act.activation(wf_hi, wf_raw, ACT.Copy).then_inc(wf_hi_ready, 1)
                elif k == 13:
                    act.wait_ge(f_step, 2)
                    act.activation(f_abs, f_lin, ACT.Abs, bias=fb_col[0:H, :]).then_inc(f_act, 1)
                    act.wait_ge(f_act, 1)
                    act.activation(f_abs, f_abs, ACT.Exp, scale=-1.0).then_inc(f_act, 1)
                    act.wait_ge(f_act, 2)
                    act.activation(f_abs, f_abs, ACT.Ln, bias=1.0).then_inc(f_act, 1)

            def head_leave(n, i, h, S):
                act.wait_ge(tile_used, n + i)
                act.wait_ge(yb_ready, h)
                for t in range(NT):
                    ins = act.activation(zb[:, t, :], ps[S][:, t, 3 * HD:4 * HD], ACT.Tanh,
                                         scale=hrstd[:, t:t + 1])
                ins.then_inc(tanh_b, 1)
                for t in range(NT):
                    ins = act.activation(vn[:, t, :], ps[S][:, t, 2 * HD:3 * HD], ACT.Copy,
                                         scale=rstd[:, t:t + 1])
                ins.then_inc(v_b, 1)

            def head_squares(h):
                act.wait_ge(qk_out, h + 1)
                act.wait_ge(probsT_psum, h)
                for t in range(NT):
                    for s in range(2):
                        ins = act.activation(probs[:, (2 * t + s) * P:(2 * t + s + 1) * P], qk[:, t, s, :],
                                             ACT.Square, scale=rstd[:, t:t + 1],
                                             accum_out=qkss[:, t, s:s + 1])
                ins.then_inc(qkss_ready, 1)

            def q_turned(h, O):
                act.wait_ge(qkT_psum, h * 2 + 1)
                act.activation(qT, ps[O][:, 0, :], ACT.Copy).then_inc(qT_ready, 1)

            def exps(h):
                for i in range(NT):
                    act.wait_ge(nmax_ready, h * NT + (i + 1))
                    act.activation(probs[:, row_at[i]:row_at[i + 1]], probs[:, row_at[i]:row_at[i + 1]],
                                   ACT.Exp, bias=nmax[:, i:i + 1], accum_out=rsum[:, i:i + 1])\
                        .then_inc(probs_ready, 1)

            def probs_turned(h, O):
                act.wait_ge(probsT_psum, h + 1)
                act.activation(probs_T[:, 0:8 * P].rearrange("p (b c) -> p b c", b=2),
                               ps[O][:, 0:2, :], ACT.Copy).then_inc(probsT_act, 1)

            def y_turned(h, O, hi):
                act.wait_ge(yT_psum, h + (G + 1))
                act.activation(hi, ps[O][:, 0, :], ACT.Copy).then_inc(yh_ready, 1)

            def b_block(n, q, off, h, S, hi, squares):
                for k in range(KC):
                    step(n, q, off + k)
                    if k == 1 and squares:
                        head_squares(h - 1)
                    elif k == 3:
                        q_turned(h - 1, 1 - S)
                    elif k == 6:
                        exps(h - 1)
                    elif k == 8:
                        probs_turned(h - 1, 1 - S)
                    elif k == 12:
                        y_turned(h - 1, 1 - S, hi)
                head_leave(n, off + KC, h, S)

            act.wait_ge(rstd_ready, 2)
            act.wait_ge(hrstd_ready, 2)
            head_leave(B0, KC, 0, 0)
            head_squares(0)
            with act.Fori(0, H // 2 - 2) as j:
                n, q = j * BPAIR + BL, j * (BPAIR // R) + BL // R
                b_block(n, q, 0, j * 2 + 1, 1, yh[:, 0, :], False)
                b_block(n, q, KC, j * 2 + 2, 0, yh[:, 1, :], True)
                for i in range(OT):
                    step(n, q, 2 * KC + i)
                    if i == 1:
                        head_squares(j * 2 + 2)
            q = BE // R
            b_block(BE, q, 0, H - 3, 1, yh[:, 0, :], False)
            b_block(BE, q, KC, H - 2, 0, yh[:, 1, :], True)
            b_block(BE, q, 2 * KC, H - 1, 1, xh[:, 0, :], True)
            for i in range(OT):
                step(BE, q, 3 * KC + i)
                if i == 1:
                    head_squares(H - 1)
                elif i == 3:
                    q_turned(H - 1, 0)
                elif i == 5:
                    exps(H - 1)
                elif i == 7:
                    probs_turned(H - 1, 0)
                    y_turned(H - 1, 0, xh[:, 1, :])
            for i in range(OT - LEAD):
                step(BE, q, 3 * KC + OT + i)

        @block.tensor
        def _(pe):
            def tile(n, i, S, hi, lo, start, stop):
                s = i % R
                pe.wait_ge(lo_ready, n + (i + 1))
                for t in range(NT):
                    a, b = hi[:, t * P:(t + 1) * P], lo[:, t * P:(t + 1) * P]
                    pe.matmul(ps[S][:, t, :], a, w_hi[:, s, :], start=start, stop=False)
                    pe.matmul(ps[S][:, t, :], a, w_lo[:, s, :], start=False, stop=False)
                    mm = pe.matmul(ps[S][:, t, :], b, w_hi[:, s, :], start=False, stop=stop)
                mm.then_inc(tile_used, 1)

            def in_tile(n, i, k, S):
                tile(n, i, S, xh[:, k, :], xl[:, k, :], k == 0, k == KC - 1)

            def turn_x(k, done):
                if k >= 4:
                    pe.wait_ge(xl_ready, done + k - 3)
                for t in range(NT):
                    mm = pe.transpose(ps[1][:, k % 4, t * P:(t + 1) * P],
                                      acc[:, t, k * P:(k + 1) * P], ident[:, :])
                mm.then_inc(xT_ready, 1)

            pe.wait_ge(const_ready, 7)
            pe.wait_ge(rows_loaded, 48)
            pe.transpose(ps[0][:, 0, 0:2 * KC + G], rows[:, :], ident[0:2 * KC + G, 0:2 * KC + G])\
                .then_inc(rows_T, 1)
            pe.wait_ge(x_loaded[0], 16)
            for k in range(4):
                turn_x(k, 0)
            pe.wait_ge(cols_ready, 1)
            for k in range(KC):
                if k + 4 < KC:
                    if k % 4 == 0:
                        pe.wait_ge(x_loaded[k // 4 + 1], 16)
                    turn_x(k + 4, 0)
                pe.wait_ge(xl_ready, k + 1)
                in_tile(0, k, k, 0)
            for k in range(KC):
                in_tile(KC, k, k, 1)
            with pe.Fori(1, VB // 2) as j:
                for S in range(2):
                    pe.wait_ge(v_out, j * (2 * NT) + (S * NT - NT))
                    for k in range(KC):
                        in_tile(j * (2 * KC), S * KC + k, k, S)

            def turn_ws(g, s, O):
                pe.wait_ge(ws_masked, g + 1)
                pe.transpose(ps[O][:, 3, 0:P], ws_raw[:, s, :], ident[:, :]).then_inc(ws_T_psum, 1)

            def turn_y(O, count):
                pe.wait_ge(y_ready, count)
                for c in range(OK):
                    for t in range(NT):
                        mm = pe.transpose(ps[O][:, c, t * P:(t + 1) * P],
                                          ug[:, t, c * P:(c + 1) * P], ident[:, :])
                mm.then_inc(yT_psum, 1)

            def mix(g, O):
                pe.wait_ge(ws_T_ready, g + 1)
                pe.wait_ge(v_normed, g + 1)
                for c in range(2):
                    mm = pe.matmul(ps[O][:, 2 + c, :], ws_T[:, :],
                                   v[:, ds(g, 1), 2 * c:2 * c + 2, :].rearrange("p g c d -> p (g c d)"),
                                   start=True, stop=True)
                mm.then_inc(mixed, 1)

            def a_block(n, off, g, S):
                O = 1 - S
                pe.wait_ge(sum_out, g * NF - 1)
                pe.wait_ge(mix_ready, g)
                for k in range(KC):
                    in_tile(n, off + k, k, S)
                    if k == 3:
                        pe.wait_ge(sum_out, g * NF)
                        pe.wait_ge(block_out, g)
                        turn_ws(g, S, O)
                        turn_y(O, g)
                    elif k == 8:
                        mix(g, O)

            def out_proj(n, off, sets, hi, lo, gates, after=()):
                for f in range(NF):
                    for gate in gates[f]:
                        pe.wait_ge(*gate)
                    for k in range(OK):
                        tile(n, off + f * OK + k, sets[f], hi[:, k, :], lo[:, k, :], k == 0, k == OK - 1)
                        for i, act_now in after:
                            if i == f * OK + k:
                                act_now()

            def a_out(n, off, g, S, count, leaves):
                out_proj(n, off, [1 - S, S, 1 - S, S], yh, yl,
                         [[(yl_ready, count)],
                          [leaves],
                          [(sum_out, g * NF + 1)],
                          [(sum_out, g * NF + 2)]])

            pe.wait_ge(v_out, NT * (VB - 1))
            for k in range(KC):
                in_tile(A0, k, k, 0)
                if k == 3:
                    pe.wait_ge(v_out, NT * VB)
                    turn_ws(0, 0, 1)
                elif k == 8:
                    mix(0, 1)
            with pe.Fori(0, G // 2 - 1) as j:
                n = j * APAIR + AL
                for e in range(2):
                    g, S, off = j * 2 + (e + 1), 1 - e, e * (KC + OT)
                    a_block(n, off, g, S)
                    pe.wait_ge(mix_ready, g + 1)
                    a_out(n, off + KC, g, S, g, (block_out, g + 1))
            g = G - 1
            a_block(AE, 0, g, 1)
            pe.wait_ge(mix_ready, g + 1)
            a_out(AE, KC, g, 1, g, (block_out, g + 1))
            pe.wait_ge(sum_out, g * NF + 3)
            turn_y(0, G)
            pe.wait_ge(sum_out, g * NF + 4)
            a_out(AE, KC + OT, G, 0, G, (yl_ready, G))

            S0 = NF * (G + 1)
            pe.wait_ge(sum_out, S0 - 1)
            for k in range(4):
                turn_x(k, KC)
            pe.wait_ge(sum_out, S0)
            for k in range(KC):
                if k + 4 < KC:
                    turn_x(k + 4, KC)
                pe.wait_ge(xl_ready, KC + k + 1)
                in_tile(B0, k, k, 0)
                if k == 12:
                    pe.wait_ge(xl_ready, 2 * KC)
                    pe.wait_ge(rstd_ready, 2)
                    for t in range(NT):
                        mm = pe.transpose(ps[1][0:H, 1, t * P:(t + 1) * P],
                                          rstd[:, t:t + 1].broadcast_to([P, H]), ident[:, :])
                    mm.then_inc(rstdT_psum, 1)
                    pe.wait_ge(wf_lo_ready, 1)
                    for c in range(KC):
                        f_hi, f_lo = wf_hi[:, c * H:(c + 1) * H], wf_lo[:, c * H:(c + 1) * H]
                        o = ps[1][0:H, 0, :]
                        pe.matmul(o, f_hi, xh[:, c, :], start=(c == 0), stop=False)
                        pe.matmul(o, f_hi, xl[:, c, :], start=False, stop=False)
                        mm = pe.matmul(o, f_lo, xh[:, c, :], start=False, stop=(c == KC - 1))
                    mm.then_inc(f_psum, 1)
            pe.wait_ge(cumT_ready, 1)
            for t in range(NT):
                mm = pe.transpose(ps[1][:, 2, t * H:(t + 1) * H], cum_T[:, t * P:(t + 1) * P],
                                  ident[0:H, 0:H])
            mm.then_inc(cumc_psum, 1)

            def turn_qk(h, O):
                pe.wait_ge(heads_out, h + 1)
                pe.wait_ge(qk_normed, h + 1)
                for s in range(2):
                    for t in range(NT):
                        mm = pe.transpose(ps[O][:, s, t * P:(t + 1) * P], qk[:, t, s, :], ident[:, :])
                    mm.then_inc(qkT_psum, 1)

            def score(h, O):
                pe.wait_ge(qT_ready, h + 1)
                pe.wait_ge(kT_ready, h + 1)
                for i in range(NT):
                    pe.matmul(ps[O][:, i, 0:(i + 1) * P], qT[:, i * P:(i + 1) * P],
                              kT[:, 0:(i + 1) * P], start=True, stop=False)
                    pe.matmul(ps[O][:, i, i * P:(i + 1) * P], ident_b[:, :], mask_b[:, :],
                              start=False, stop=True).then_inc(scores, 1)

            def turn_probs(h, O):
                pe.wait_ge(probs_ready, h * NT + NT)
                for b in range(NB):
                    mm = pe.transpose(ps[O][:, b // 4, b % 4 * P:(b % 4 + 1) * P],
                                      probs[:, b * P:(b + 1) * P], ident[:, :])
                mm.then_inc(probsT_psum, 1)

            def attend(h, O):
                pe.wait_ge(probsT_act, h + 1)
                pe.wait_ge(probsT_dve, h + 1)
                for i in range(NT):
                    for c in range(i + 1):
                        b = row_at[i] + c * P
                        mm = pe.matmul(ps[O][:, 3, i * P:(i + 1) * P], probs_T[:, b:b + P],
                                       vn[:, c, :], start=(c == 0), stop=(c == i))
                mm.then_inc(attended, 1)

            def turn_yb(h, O):
                pe.wait_ge(yb_ready, h + 1)
                for t in range(NT):
                    mm = pe.transpose(ps[O][:, 0, t * P:(t + 1) * P], yb[:, t, :], ident[:, :])
                mm.then_inc(yT_psum, 1)

            def b_block(n, off, h, S, added=None):
                for k in range(KC):
                    in_tile(n, off + k, k, S)
                    if k == 3 and added is not None:
                        pe.wait_ge(sum_out, added)
                    elif k == 4:
                        turn_qk(h - 1, 1 - S)
                    elif k == 6:
                        score(h - 1, 1 - S)
                    elif k == 9:
                        turn_probs(h - 1, 1 - S)
                    elif k == 11:
                        attend(h - 1, 1 - S)
                    elif k == 13:
                        turn_yb(h - 1, 1 - S)

            pe.wait_ge(cumc_ready, 1)
            with pe.Fori(0, H // 2 - 2) as j:
                n = j * BPAIR + BL
                pe.wait_ge(sum_out, j * NF + (S0 - 1))
                b_block(n, 0, j * 2 + 1, 1, added=j * NF + S0)
                pe.wait_ge(yl_ready, j * 2 + (G + 1))
                b_block(n, KC, j * 2 + 2, 0)
                out_proj(n, 2 * KC, [1, 0, 1, 0], yh, yl,
                         [[(yl_ready, j * 2 + (G + 2))],
                          [(heads_out, j * 2 + 3)],
                          [(sum_out, j * NF + (S0 + 1))],
                          [(sum_out, j * NF + (S0 + 2))]])
            S1 = S0 + (H // 2 - 2) * NF
            pe.wait_ge(sum_out, S1 - 1)
            b_block(BE, 0, H - 3, 1, added=S1)
            pe.wait_ge(yl_ready, G + H - 3)
            b_block(BE, KC, H - 2, 0)
            pe.wait_ge(yl_ready, G + H - 2)
            b_block(BE, 2 * KC, H - 1, 1)
            h = H - 1
            out_proj(BE, 3 * KC, [0, 1, 1, 1], yh, yl,
                     [[(yl_ready, G + H - 1)],
                      [(heads_out, H)],
                      [(sum_out, S1 + 2)],
                      [(sum_out, S1 + 3)]],
                     after=[(3, lambda: pe.wait_ge(sum_out, S1 + 1)),
                            (3, lambda: turn_qk(h, 0)), (4, lambda: score(h, 0)),
                            (6, lambda: turn_probs(h, 0)), (7, lambda: attend(h, 0)),
                            (7, lambda: turn_yb(h, 0))])
            out_proj(BE, 3 * KC + OT, [0, 1, 0, 1], xh, xl,
                     [[(yl_ready, G + H)],
                      [(sum_out, S1 + 4)],
                      [(sum_out, S1 + 5)],
                      [(sum_out, S1 + 6)]])

        @block.vector
        def _(dve):
            def split(n, i):
                s = i % R
                dve.wait_ge(hi_ready, n + (i + 1))
                dve.tensor_tensor(w_lo[:, s, :], w_raw[:, s, :], w_hi[:, s, :].bitcast(F32),
                                  ALU.subtract).then_inc(lo_ready, 1)

            def step(n, i):
                split(n, i + LEAD)

            def x_low(k, gain, done):
                dve.wait_ge(xh_ready, done + k + 1)
                dve.scalar_tensor_tensor(xl[:, k, :], ps[1][:, k % 4, :], gain[:, k:k + 1],
                                         xh[:, k, :].bitcast(F32), ALU.mult, ALU.subtract)\
                    .then_inc(xl_ready, 1)

            def x_stats(layer):
                dve.wait_ge(ssx_ready, (layer + 1) * NT)
                dve.tensor_scalar(msx[:, :], ssx[:, :], 1.0 / D, EPS, ALU.mult, ALU.add)\
                    .then_inc(msx_ready, 1)
                dve.wait_ge(rstd_ready, layer + 1)
                dve.tensor_scalar(hrstd[:, :], rstd[:, :], 0.5, None, ALU.mult).then_inc(hrstd_ready, 1)

            dve.wait_ge(rows_T, 1)
            dve.tensor_copy(cols[:, :], ps[0][:, 0, 0:2 * KC + G]).then_inc(cols_ready, 1)
            dve.wait_ge(cols_ready, 1)
            for k in range(4):
                x_low(k, a_gain, 0)
                if k < LEAD:
                    split(0, k)
            for k in range(KC):
                if k + 4 < KC:
                    x_low(k + 4, a_gain, 0)
                step(0, k)
            x_stats(0)
            for k in range(KC):
                step(KC, k)
            with dve.Fori(1, VB // 2) as j:
                for k in range(2 * KC):
                    step(j * (2 * KC), k)

            def v_norm(g, s, count):
                dve.wait_ge(vg_loaded[s], count)
                for c in range(NT):
                    a = v[:, ds(g, 1), c, :].rearrange("p g d -> p (g d)")
                    ins = dve.scalar_tensor_tensor(a, a, vrstd[:, c:c + 1], vg_row[:, s, :],
                                                   ALU.mult, ALU.mult)
                ins.then_inc(v_normed, 1)

            def ws_leave(g, O):
                dve.wait_ge(ws_T_psum, g + 1)
                dve.tensor_copy(ws_T[:, :], ps[O][:, 3, 0:P]).then_inc(ws_T_ready, 1)

            def mix_leave(g, O):
                dve.wait_ge(mixed, g + 1)
                dve.tensor_scalar(v[:, ds(g, 1), :, :].rearrange("p g c d -> p (g c d)"),
                                  ps[O][:, 2:4, :].rearrange("p b c -> p (b c)"),
                                  b_s_cols[:, ds(g, 1)], None, ALU.add).then_inc(mix_ready, 1)

            def y_low(O, count):
                dve.wait_ge(yh_ready, count)
                dve.tensor_tensor(yl[:, :, :], ps[O][:, 0:OK, :], yh[:, :, :].bitcast(F32),
                                  ALU.subtract).then_inc(yl_ready, 1)

            def leave(g, S):
                dve.wait_ge(u_ready, g + 1)
                dve.wait_ge(mix_ready, g + 1)
                dve.tensor_tensor(ug[:, :, :], ug[:, :, :],
                                  v[:, ds(g, 1), :, :].rearrange("p g c d -> p (g c) d"), ALU.mult)\
                    .then_inc(gate_step, 1)
                dve.wait_ge(tanh_ready, g + 1)
                dve.scalar_tensor_tensor(zz[:, :, :], zz[:, :, :], 1.0, ps[S][:, :, GD:2 * GD],
                                         ALU.add, ALU.mult).then_inc(block_out, 1)
                dve.wait_ge(gate_step, g + 1)
                dve.wait_ge(block_out, g + 1)
                for t in range(NT):
                    ins = dve.scalar_tensor_tensor(ug[:, t, :], ug[:, t, :], hrstd[:, t:t + 1], zz[:, t, :],
                                                   ALU.mult, ALU.mult)
                ins.then_inc(y_ready, 1)

            def a_block(n, off, g, S, loads):
                for k in range(KC):
                    step(n, off + k)
                    if k == 0:
                        v_norm(g, S, loads)
                    elif k == 2:
                        ws_leave(g, 1 - S)
                        y_low(1 - S, g)
                    elif k == 7:
                        mix_leave(g, 1 - S)
                leave(g, S)

            def add_out(n, i, f, S):
                dve.wait_ge(tile_used, n + i)
                for b in range(2):
                    o = acc[:, 2 * b:2 * b + 2, f * FB:(f + 1) * FB]
                    ins = dve.tensor_tensor(o, ps[S][:, 2 * b:2 * b + 2, :], o, ALU.add)
                ins.then_inc(sum_out, 1)

            def out_steps(n, off, sets):
                for i in range(OT):
                    step(n, off + i)
                    if i % OK == OK - 1:
                        add_out(n, off + i + 1, i // OK, sets[i // OK])

            for k in range(KC):
                step(A0, k)
                if k == 1:
                    dve.wait_ge(vsq_ready, NT * VB)
                    dve.tensor_reduce(vms[:, 0, :], vsq[:, :, :], AX.X, ALU.add).then_inc(vms_ready, 1)
                    dve.wait_ge(vms_ready, 1)
                    dve.tensor_scalar(vms[:, 1, :], vms[:, 0, :], 1.0 / AW, EPS, ALU.mult, ALU.add)\
                        .then_inc(vms_ready, 1)
                elif k == 2:
                    ws_leave(0, 1)
                elif k == 4:
                    dve.wait_ge(vrstd_ready, 1)
                    v_norm(0, 0, 16)
                elif k == 7:
                    dve.wait_ge(v_out, NT * VB)
                    dve.tensor_copy(vms[:, 0, :], vrstd[:, :]).then_inc(sum_out, NF)
                    mix_leave(0, 1)
            leave(0, 0)
            with dve.Fori(0, G // 2 - 1) as j:
                n = j * APAIR + AL
                a_block(n, 0, j * 2 + 1, 1, j * 16 + 16)
                out_steps(n, KC, [0, 1, 0, 1])
                a_block(n, KC + OT, j * 2 + 2, 0, j * 16 + 32)
                out_steps(n, 2 * KC + OT, [1, 0, 1, 0])
            a_block(AE, 0, G - 1, 1, 8 * G)
            out_steps(AE, KC, [0, 1, 0, 1])
            y_low(0, G)
            out_steps(AE, KC + OT, [1, 0, 1, 0])

            for k in range(4):
                x_low(k, b_gain, KC)
            for k in range(KC):
                if k + 4 < KC:
                    x_low(k + 4, b_gain, KC)
                step(B0, k)
                if k == 10:
                    dve.wait_ge(wf_hi_ready, 1)
                    dve.tensor_tensor(wf_lo, wf_raw, wf_hi.bitcast(F32), ALU.subtract)\
                        .then_inc(wf_lo_ready, 1)
                elif k == 11:
                    x_stats(1)
                    dve.wait_ge(gains_loaded, 48)
                    dve.tensor_scalar(qg_row, qg_row, SCALE, None, ALU.mult).then_inc(gains_ready, 1)
                elif k == 13:
                    dve.wait_ge(rstdT_psum, 1)
                    dve.tensor_copy(rstd_row, ps[1][0:H, 1, :]).then_inc(f_step, 1)
                    dve.wait_ge(f_psum, 1)
                    dve.wait_ge(f_step, 1)
                    dve.tensor_tensor(f_lin, ps[1][0:H, 0, :], rstd_row, ALU.mult).then_inc(f_step, 1)
                    dve.wait_ge(f_step, 2)
                    dve.tensor_scalar(f_min, f_lin, fb_col[0:H, :], 0.0, ALU.add, ALU.min)\
                        .then_inc(f_step, 1)
                elif k == 14:
                    dve.wait_ge(f_act, 3)
                    dve.wait_ge(f_step, 3)
                    dve.tensor_tensor(f_log, f_min, f_abs, ALU.subtract).then_inc(f_step, 1)
                    dve.wait_ge(f_step, 4)
                    dve.wait_ge(const_ready, 8)
                    dve.tensor_tensor_scan(cum_T, f_one, f_log, 0.0, ALU.mult, ALU.add)\
                        .then_inc(cumT_ready, 1)
            dve.wait_ge(cumc_psum, 1)
            dve.tensor_copy(cum_col[:, :, :], ps[1][:, 2, 0:NT * H].rearrange("p (t h) -> p t h", t=NT))\
                .then_inc(cumc_ready, 1)
            dve.wait_ge(cumc_ready, 1)
            dve.wait_ge(gains_ready, 1)

            def head_leave(n, i, h, S):
                dve.wait_ge(tile_used, n + i)
                dve.wait_ge(tanh_b, h + 1)
                dve.wait_ge(v_b, h + 1)
                dve.tensor_copy(qk[:, :, :, :].rearrange("p t s d -> p t (s d)"),
                                ps[S][:, :, 0:2 * HD]).then_inc(qk_out, 1)
                dve.scalar_tensor_tensor(zb[:, :, :], zb[:, :, :], 1.0, ps[S][:, :, 3 * HD:4 * HD],
                                         ALU.add, ALU.mult).then_inc(heads_out, 1)

            def head_means(h):
                dve.wait_ge(qkss_ready, h + 1)
                dve.tensor_scalar(qkms[:, :, :], qkss[:, :, :], 1.0 / HD, EPS, ALU.mult, ALU.add)\
                    .then_inc(qkms_ready, 1)

            def head_norm(h):
                dve.wait_ge(qkr_ready, h + 1)
                for s in range(2):
                    ins = dve.tensor_tensor(qkr[:, :, s], qkr[:, :, s], rstd[:, :], ALU.mult)
                ins.then_inc(qkr_scaled, 1)
                dve.wait_ge(qkr_scaled, h + 1)
                for t in range(NT):
                    for s, g in ((0, qg_row), (1, kg_row)):
                        ins = dve.scalar_tensor_tensor(qk[:, t, s, :], qk[:, t, s, :], qkr[:, t, s:s + 1], g,
                                                       ALU.mult, ALU.mult)
                ins.then_inc(qk_normed, 1)

            def k_turned(h, O):
                dve.wait_ge(qkT_psum, h * 2 + 2)
                dve.tensor_copy(kT, ps[O][:, 1, :]).then_inc(kT_ready, 1)

            def row_logits(h, i, O, s):
                dve.wait_ge(scores, h * NT + (i + 1))
                p = probs[:, row_at[i]:row_at[i + 1]]
                dve.scalar_tensor_tensor(p, ps[O][:, i, 0:(i + 1) * P],
                                         cum_col[:, i, ds(h, 1)], cum_row[:, s, 0:(i + 1) * P],
                                         ALU.add, ALU.subtract).then_inc(logits, 1)
                dve.wait_ge(logits, h * NT + (i + 1))
                dve.tensor_reduce(nmax[:, i:i + 1], p, AX.X, ALU.max, negate=True).then_inc(nmax_ready, 1)

            def probs_turned(h, O):
                dve.wait_ge(probsT_psum, h + 1)
                dve.tensor_copy(probs_T[:, 8 * P:NB * P], ps[O][:, 2, 0:(NB - 8) * P])\
                    .then_inc(probsT_dve, 1)
                dve.wait_ge(probs_ready, h * NT + NT)
                dve.reciprocal(rsum[:, :], rsum[:, :]).then_inc(rinv_ready, 1)
                dve.wait_ge(rinv_ready, h * 2 + 1)
                dve.tensor_tensor(rinv[:, :], rsum[:, :], hrstd[:, :], ALU.mult).then_inc(rinv_ready, 1)

            def gate_head(h, O):
                dve.wait_ge(attended, h + 1)
                dve.wait_ge(rinv_ready, h * 2 + 2)
                for i in range(NT):
                    ins = dve.scalar_tensor_tensor(yb[:, i, :], ps[O][:, 3, i * P:(i + 1) * P],
                                                   rinv[:, i:i + 1], zb[:, i, :], ALU.mult, ALU.mult)
                ins.then_inc(yb_ready, 1)

            def y_turned(h, O, hi, lo):
                dve.wait_ge(yh_ready, h + (G + 1))
                dve.tensor_tensor(lo, ps[O][:, 0, :], hi.bitcast(F32), ALU.subtract).then_inc(yl_ready, 1)

            def b_block(n, off, h, S, s, loads, hi, lo, norm):
                for k in range(KC):
                    step(n, off + k)
                    if k == 1 and norm:
                        head_means(h - 1)
                    elif k == 2 and norm:
                        head_norm(h - 1)
                    elif k == 3:
                        k_turned(h - 1, 1 - S)
                    elif k == 5:
                        dve.wait_ge(cum_loaded[s], loads)
                        row_logits(h - 1, 0, 1 - S, s)
                        row_logits(h - 1, 1, 1 - S, s)
                    elif k == 6:
                        row_logits(h - 1, 2, 1 - S, s)
                        row_logits(h - 1, 3, 1 - S, s)
                    elif k == 8:
                        probs_turned(h - 1, 1 - S)
                    elif k == 10:
                        gate_head(h - 1, 1 - S)
                    elif k == 12:
                        y_turned(h - 1, 1 - S, hi, lo)
                head_leave(n, off + KC, h, S)

            y0, y1 = (yh[:, 0, :], yl[:, 0, :]), (yh[:, 1, :], yl[:, 1, :])
            head_leave(B0, KC, 0, 0)
            head_means(0)
            head_norm(0)
            with dve.Fori(0, H // 2 - 2) as j:
                n = j * BPAIR + BL
                b_block(n, 0, j * 2 + 1, 1, 0, j * 16 + 16, *y0, False)
                b_block(n, KC, j * 2 + 2, 0, 1, j * 16 + 16, *y1, True)
                for i in range(OT):
                    step(n, 2 * KC + i)
                    if i == 1:
                        head_means(j * 2 + 2)
                    if i % OK == OK - 1:
                        add_out(n, 2 * KC + i + 1, i // OK, (1, 0, 1, 0)[i // OK])
                    if i == 5:
                        head_norm(j * 2 + 2)
            b_block(BE, 0, H - 3, 1, 0, 8 * (H - 2), *y0, False)
            b_block(BE, KC, H - 2, 0, 1, 8 * (H - 2), *y1, True)
            b_block(BE, 2 * KC, H - 1, 1, 0, 8 * H, xh[:, 0, :], xl[:, 0, :], True)
            for i in range(OT):
                step(BE, 3 * KC + i)
                if i == 1:
                    head_means(H - 1)
                elif i == 2:
                    head_norm(H - 1)
                if i % OK == OK - 1:
                    add_out(BE, 3 * KC + i + 1, i // OK, (0, 1, 1, 1)[i // OK])
                if i == 3:
                    k_turned(H - 1, 0)
                elif i == 4:
                    dve.wait_ge(cum_loaded[1], 8 * H)
                    for r in range(NT):
                        row_logits(H - 1, r, 0, 1)
            probs_turned(H - 1, 0)
            gate_head(H - 1, 0)
            y_turned(H - 1, 0, xh[:, 1, :], xl[:, 1, :])
            for i in range(OT):
                if i < OT - LEAD:
                    step(BE, 3 * KC + OT + i)
                if i % OK == OK - 1:
                    add_out(BE, 3 * KC + OT + i + 1, i // OK, i // OK % 2)


_INS = ["x", "a_norm_g", "a_w_in", "a_v_norm_g", "a_w_s", "a_b_s", "a_w_out",
        "b_norm_g", "b_w_in", "b_f_bias", "b_q_norm_g", "b_k_norm_g", "b_w_out"]


def kernel(**inputs):
    import numpy as _np
    import concourse.bacc as _bacc
    from concourse import mybir as _mybir
    from concourse.bass_utils import run_bass_kernel_spmd as _run

    nc = _bacc.Bacc("TRN2", target_bir_lowering=False, num_devices=1)
    arrays, args = {}, []
    for name in _INS:
        a = _np.ascontiguousarray(inputs[name])
        arrays[f"in_{name}_dram"] = a
        args.append(nc.dram_tensor(f"in_{name}_dram", a.shape, _mybir.dt.from_np(a.dtype),
                                   kind="ExternalInput").ap())
    out = nc.dram_tensor("out_dram", inputs["x"].shape, _mybir.dt.float32, kind="ExternalOutput").ap()
    build_trunk(nc, *args, out)
    r = _run(nc, [arrays], core_ids=[0])
    return r.results[0]["out_dram"]
```

```python
from contextlib import ExitStack

import concourse.bass as bass
from concourse import mybir

F32 = mybir.dt.float32
F32R = mybir.dt.float32r
BF16 = mybir.dt.bfloat16
ACT = mybir.ActivationFunctionType
ALU = mybir.AluOpType
AX = mybir.AxisListType
ds = bass.ds

P = 128
EPS = 1e-6


def build_trunk(nc, x, a_norm_g, a_w_in, a_v_norm_g, a_w_s, a_b_s, a_w_out,
                b_norm_g, b_w_in, b_f_bias, b_q_norm_g, b_k_norm_g, b_w_out, out):
    SEQ, D = x.shape[1], x.shape[2]
    NT = SEQ // P
    KC = D // P
    AW = a_w_out.shape[1]
    G = a_w_s.shape[1]
    GD = AW // G
    H = b_f_bias.shape[1]
    HD = b_q_norm_g.shape[1]
    FB = 512
    NF = D // FB
    VB = AW // FB
    R = 4
    LEAD = R - 1
    X1 = FB // P
    OK = GD // P
    assert (NT, NF, GD, HD, OK, SEQ) == (4, 4, 256, P, 2, 512) and G == H == 16 == KC
    OT = NF * OK
    SCALE = float(HD) ** -0.5
    NEG = -1e30

    A0 = VB * KC
    AL = A0 + KC
    APAIR = 2 * (KC + OT)
    AE = AL + (G // 2 - 1) * APAIR
    B0 = AE + KC + 2 * OT
    BL = B0 + KC
    BPAIR = 2 * KC + OT
    BE = BL + (H // 2 - 2) * BPAIR
    LAST_BLOCKS = [(0, 0, [H - 4, H - 3]), (1, 1, [H - 4, H - 3, H - 2]),
                   (2, 1, [H - 4, H - 3, H - 2]), (3, 1, [H - 4, H - 3]),
                   (0, 1, [H - 2, H - 1]), (1, 0, [H - 1]), (2, 1, [H - 1]), (3, 0, [H - 2, H - 1])]
    LAST = sum(len(b[2]) for b in LAST_BLOCKS)
    assert LAST == NF * 4
    assert A0 % R == AL % R == APAIR % R == AE % R == B0 % R == BPAIR % R == 0

    x_t = x[0].rearrange("(t p) d -> p t d", p=P)
    out_t = out[0].rearrange("(t p) d -> p t d", p=P)
    a_in = a_w_in[0]
    a_uz = a_w_in[0].rearrange("r (s c) -> r s c", s=3)[:, 0:3:2, :]
    a_out = a_w_out[0]
    b_qkvz = b_w_in[0][:, 0:4 * D].rearrange("r (s c) -> r s c", s=4)
    b_f = b_w_in[0][:, 4 * D:4 * D + H].rearrange("(k p) h -> p k h", p=P)
    b_out = b_w_out[0]
    cum_dram = nc.dram_tensor("cum_rows", [H, SEQ], F32).ap()

    with ExitStack() as ctx:
        def sb(name, shape, dt=F32):
            return ctx.enter_context(nc.sbuf_tensor(name, shape, dt))

        def sem(name):
            return ctx.enter_context(nc.semaphore(name))

        acc = sb("acc", [P, NT, D])
        xh = sb("xh", [P, KC, SEQ], F32R)
        xl = sb("xl", [P, KC, SEQ], F32R)
        v_all = sb("v_all", [P, G * NT * GD])
        v = v_all[:, :].rearrange("p (g c d) -> p g c d", g=G, c=NT)
        yh = sb("yh", [P, OK, SEQ], F32R)
        yl = sb("yl", [P, OK, SEQ], F32R)
        ug = sb("ug", [P, OK, SEQ])
        zz = sb("zz", [P, OK, SEQ])
        ug_v, zz_v = (m[:, :, :].rearrange("p b (c d) -> p (b c) d", d=GD) for m in (ug, zz))
        w_raw = sb("w_raw", [P, R, FB])
        w_hi = sb("w_hi", [P, R, FB], F32R)
        w_lo = sb("w_lo", [P, R, FB], F32R)
        ident = sb("ident", [P, P])
        ident_b = sb("ident_b", [P, P], BF16)
        mask_b = sb("mask_b", [P, P], BF16)
        ws_raw = sb("ws_raw", [P, 2, P])
        ws_T = sb("ws_T", [P, P])
        vg_row = sb("vg_row", [P, GD])
        bs_row = sb("bs_row", [P, P])
        rstd_bc = sb("rstd_bc", [P, SEQ])
        a_rows = sb("a_rows", [KC, P])
        b_rows = sb("b_rows", [KC, P])
        a_gain = sb("a_gain", [P, KC])
        b_gain = sb("b_gain", [P, KC])
        mhalf = sb("mhalf", [P, 2 * NT])
        ssx = sb("ssx", [P, NT])
        msx = sb("msx", [P, NT])
        rstd = sb("rstd", [P, NT])
        hrstd = sb("hrstd", [P, NT])
        vsq = sb("vsq", [P, NT, VB])
        vms = sb("vms", [P, 2, NT])
        vrstd = sb("vrstd", [P, NT])
        qkss = sb("qkss", [P, NT, 2])
        qkms = sb("qkms", [P, NT, 2])
        qkr = sb("qkr", [P, NT, 2])
        nmax = sb("nmax", [P, NT])
        first_use = sb("first_use", [P, 1])
        rsum = sb("rsum", [P, NT])
        rinv = sb("rinv", [P, NT])

        at = [0]

        def part(n, pattern=None, **sizes):
            ap = v_all[:, at[0]:at[0] + n]
            at[0] += n
            return ap.rearrange(pattern, **sizes) if pattern else ap

        qk = part(NT * 2 * HD, "p (t s d) -> p t s d", t=NT, s=2)
        vn = part(NT * HD, "p (t d) -> p t d", t=NT)
        zb = part(NT * HD, "p (t d) -> p t d", t=NT)
        yb = part(NT * HD, "p (t d) -> p t d", t=NT)
        qT = part(SEQ)
        kT = part(SEQ)
        NB = NT * (NT + 1) // 2
        probs = part(NB * P)
        probs_T = part(NB * P)
        cum_row = part(2 * SEQ, "p (b s) -> p b s", b=2)
        qg_row = part(HD)
        kg_row = part(HD)
        fb_col = part(1)
        wf_raw = part(KC * H)
        rstd_row, f_lin, f_abs, f_min, f_log, f_one, cum_T = (part(SEQ)[0:H, :] for _ in range(7))
        cum_col = part(NT * H, "p (t h) -> p t h", t=NT)
        junk = part(D)
        row_at = [i * (i + 1) // 2 * P for i in range(NT + 1)]
        assert at[0] <= G * NT * GD
        y_last, y_last_lo = xh[:, KC - OK:, :], xl[:, KC - OK:, :]
        wf_hi, wf_lo = yh[:, 0, 0:KC * H], yl[:, 0, 0:KC * H]

        ps = [ctx.enter_context(nc.psum_tensor(f"ps{i}", [P, 4, 512], F32)) for i in range(2)]

        w_loaded = [sem(f"w_loaded{s}") for s in range(R)]
        hi_ready = sem("hi_ready")
        lo_ready = sem("lo_ready")
        tile_used = sem("tile_used")
        x_loaded = [sem(f"x_loaded{c}") for c in range(X1 + NF - 1)]
        a_rows_loaded = sem("a_rows_loaded")
        b_rows_loaded = sem("b_rows_loaded")
        const_ready = sem("const_ready")
        rows_T = sem("rows_T")
        gain_ready = sem("gain_ready")
        xT_ready = sem("xT_ready")
        xh_ready = sem("xh_ready")
        xl_ready = sem("xl_ready")
        ssx_ready = sem("ssx_ready")
        msx_ready = sem("msx_ready")
        rstd_ready = sem("rstd_ready")
        hrstd_ready = sem("hrstd_ready")
        v_out = sem("v_out")
        vsq_ready = sem("vsq_ready")
        vms_ready = sem("vms_ready")
        vrstd_ready = sem("vrstd_ready")
        ws_loaded = [sem("ws_loaded0"), sem("ws_loaded1")]
        vg_loaded = sem("vg_loaded")
        bs_loaded = sem("bs_loaded")
        bc_psum = sem("bc_psum")
        bc_ready = sem("bc_ready")
        mask_turn = sem("mask_turn")
        ws_masked = sem("ws_masked")
        ws_T_psum = sem("ws_T_psum")
        ws_T_ready = sem("ws_T_ready")
        v_normed = sem("v_normed")
        mixed = sem("mixed")
        mix_ready = sem("mix_ready")
        z_scaled = sem("z_scaled")
        u_scaled = sem("u_scaled")
        gelu_ready = sem("gelu_ready")
        tanh_ready = sem("tanh_ready")
        block_out = sem("block_out")
        gate_step = sem("gate_step")
        y_ready = sem("y_ready")
        yT_psum = sem("yT_psum")
        yh_ready = sem("yh_ready")
        yl_ready = sem("yl_ready")
        sum_out = sem("sum_out")
        heads_out = sem("heads_out")
        qk_out = sem("qk_out")
        tanh_b = sem("tanh_b")
        v_b = sem("v_b")
        qkss_ready = sem("qkss_ready")
        qkms_ready = sem("qkms_ready")
        qkr_ready = sem("qkr_ready")
        qkr_scaled = sem("qkr_scaled")
        qk_normed = sem("qk_normed")
        qkT_psum = sem("qkT_psum")
        qT_ready = sem("qT_ready")
        kT_ready = sem("kT_ready")
        scores = sem("scores")
        logits = sem("logits")
        nmax_ready = sem("nmax_ready")
        probs_ready = sem("probs_ready")
        rinv_ready = sem("rinv_ready")
        probsT_psum = sem("probsT_psum")
        probsT_act = sem("probsT_act")
        probsT_dve = sem("probsT_dve")
        attended = sem("attended")
        yb_ready = sem("yb_ready")
        gains_loaded = sem("gains_loaded")
        gains_ready = sem("gains_ready")
        wf_loaded = sem("wf_loaded")
        wf_hi_ready = sem("wf_hi_ready")
        wf_lo_ready = sem("wf_lo_ready")
        f_psum = sem("f_psum")
        f_step = sem("f_step")
        f_act = sem("f_act")
        rstdT_psum = sem("rstdT_psum")
        cumT_ready = sem("cumT_ready")
        cum_stored = sem("cum_stored")
        cumc_psum = sem("cumc_psum")
        cumc_ready = sem("cumc_ready")
        cum_loaded = [sem("cum_loaded0"), sem("cum_loaded1")]
        bank_done = sem("bank_done")
        bank_added = sem("bank_added")
        out_stored = sem("out_stored")

        block = ctx.enter_context(nc.Block())

        @block.sync
        def _(sp):
            def load(n, i, src, first=False):
                s = i % R
                if not first:
                    sp.wait_ge(lo_ready, n + (i - R + 1))
                dst = w_raw[:, s, :]
                if len(src.shape) == 3:
                    dst = dst.rearrange("p (s c) -> p s c", s=src.shape[1])
                sp.dma_start(dst, src).then_inc(w_loaded[s], 16)

            def v_block(n, b):
                for k in range(KC):
                    load(n, k, a_in[k * P:(k + 1) * P, ds(AW + b * FB, FB)])

            def a_block(n, off, g):
                for k in range(KC):
                    load(n, off + k, a_uz[k * P:(k + 1) * P, :, ds(g * GD, GD)])

            def out_proj(n, off, w, row):
                for f in range(NF):
                    for k in range(OK):
                        load(n, off + f * OK + k, w[ds(row + k * P, P), f * FB:(f + 1) * FB])

            def b_block(n, off, h):
                for k in range(KC):
                    load(n, off + k, b_qkvz[k * P:(k + 1) * P, :, ds(h * HD, HD)])

            def load_x(c):
                cols_c = slice(c * P, (c + 1) * P) if c < X1 else slice((c - X1 + 1) * FB, (c - X1 + 2) * FB)
                sp.dma_start(acc[:, :, cols_c], x_t[:, :, cols_c]).then_inc(x_loaded[c], 16)

            for k in range(KC):
                if k < X1 + NF - 1:
                    load_x(k)
                load(0, k, a_in[k * P:(k + 1) * P, AW:AW + FB], first=k < R)
            v_block(KC, 1)
            with sp.Fori(1, VB // 2) as j:
                v_block(j * (2 * KC), j * 2)
                v_block(j * (2 * KC) + KC, j * 2 + 1)
            a_block(A0, 0, 0)
            with sp.Fori(0, G // 2 - 1) as j:
                n = j * APAIR + AL
                a_block(n, 0, j * 2 + 1)
                out_proj(n, KC, a_out, j * (2 * GD))
                a_block(n, KC + OT, j * 2 + 2)
                out_proj(n, 2 * KC + OT, a_out, j * (2 * GD) + GD)
            a_block(AE, 0, G - 1)
            out_proj(AE, KC, a_out, (G - 2) * GD)
            out_proj(AE, KC + OT, a_out, (G - 1) * GD)
            b_block(B0, 0, 0)
            with sp.Fori(0, H // 2 - 2) as j:
                n = j * BPAIR + BL
                b_block(n, 0, j * 2 + 1)
                b_block(n, KC, j * 2 + 2)
                out_proj(n, 2 * KC, b_out, j * (2 * HD))
            for e in range(3):
                b_block(BE, e * KC, H - 3 + e)
            i = 3 * KC
            for f, S, heads in LAST_BLOCKS:
                for h in heads:
                    load(BE, i, b_out[h * HD:(h + 1) * HD, f * FB:(f + 1) * FB])
                    i += 1
            for f in range(NF - 1):
                sp.wait_ge(bank_added, (NF + f + 1) * NT)
                sp.dma_start(out_t[:, :, f * FB:(f + 1) * FB],
                             acc[:, :, f * FB:(f + 1) * FB]).then_inc(out_stored, 16)
            for t in range(NT):
                sp.wait_ge(bank_added, (2 * NF - 1) * NT + t + 1)
                sp.dma_start(out_t[:, t, D - FB:D], acc[:, t, D - FB:D]).then_inc(out_stored, 16)
            sp.wait_ge(out_stored, 16 * (NF - 1 + NT))

        @block.gpsimd
        def _(pool):
            pool.memset(ident[:, :], 0.0).then_inc(const_ready, 1)
            pool.memset(ident_b[:, :], 0.0).then_inc(const_ready, 1)
            pool.memset(mask_b[:, :], 0.0).then_inc(const_ready, 1)
            pool.memset(mhalf[:, :], -0.5).then_inc(const_ready, 1)
            pool.wait_ge(const_ready, 4)
            for m in (ident, ident_b):
                pool.affine_select(out=m[:, :], in_=m[:, :], compare_op=ALU.not_equal, fill=1.0,
                                   base=0, pattern=[[-1, P]], channel_multiplier=1).then_inc(const_ready, 1)
            pool.affine_select(out=mask_b[:, :], in_=mask_b[:, :], compare_op=ALU.is_ge, fill=NEG,
                               base=0, pattern=[[-1, P]], channel_multiplier=1).then_inc(const_ready, 1)

            def power(dst, src, n):
                return pool.tensor_tensor(dst, src, mhalf[:, 0:n], ALU.pow)

            pool.wait_ge(msx_ready, 1)
            power(rstd[:, :], msx[:, :], NT).then_inc(rstd_ready, 1)

            def load_group(g, s, first=False):
                if not first:
                    pool.wait_ge(ws_T_psum, g - 1)
                pool.dma_start(ws_raw[:, s, :], a_w_s[0, ds(g, 1)].rearrange("a t s -> t (a s)"))\
                    .then_inc(ws_loaded[s], 16)

            def load_rows(g, first=False):
                if not first:
                    pool.wait_ge(v_normed, g)
                pool.dma_start(vg_row[:, :], a_v_norm_g[0:1, ds(g * GD, GD)].broadcast_to([P, GD]))\
                    .then_inc(vg_loaded, 16)
                if not first:
                    pool.wait_ge(mix_ready, g)
                pool.dma_start(bs_row[:, :], a_b_s[0, ds(g, 1)].broadcast_to([P, P]))\
                    .then_inc(bs_loaded, 16)

            def mask_group(g, s, count):
                pool.wait_ge(ws_loaded[s], count)
                pool.sem_inc(mask_turn, 1)
                pool.affine_select(out=ws_raw[:, s, :], in_=ws_raw[:, s, :], compare_op=ALU.is_ge,
                                   fill=0.0, base=0, pattern=[[-1, P]], channel_multiplier=1)\
                    .then_inc(ws_masked, 1)

            load_group(0, 0, first=True)
            load_group(1, 1, first=True)
            load_rows(0, first=True)
            mask_group(0, 0, 16)
            pool.wait_ge(vms_ready, 2)
            power(vrstd[:, :], vms[:, 1, :], NT).then_inc(vrstd_ready, 1)
            mask_group(1, 1, 16)
            load_rows(1)
            with pool.Fori(1, G // 2) as j:
                for s in range(2):
                    load_group(j * 2 + s, s)
                    mask_group(j * 2 + s, s, j * 16 + 16)
                    load_rows(j * 2 + s)

            pool.wait_ge(y_ready, G)
            pool.dma_start(qg_row, b_q_norm_g[0:1, :].broadcast_to([P, HD])).then_inc(gains_loaded, 16)
            pool.dma_start(kg_row, b_k_norm_g[0:1, :].broadcast_to([P, HD])).then_inc(gains_loaded, 16)
            pool.dma_start(fb_col[0:H, :], b_f_bias.rearrange("a h -> h a")).then_inc(gains_loaded, 16)
            pool.dma_start(wf_raw.rearrange("p (k h) -> p k h", h=H), b_f).then_inc(wf_loaded, 16)
            pool.memset(f_one, 1.0).then_inc(const_ready, 1)
            pool.wait_ge(msx_ready, 2)
            pool.wait_ge(hrstd_ready, 1)
            power(rstd[:, :], msx[:, :], NT).then_inc(rstd_ready, 1)
            pool.wait_ge(cumT_ready, 1)
            pool.dma_start(cum_dram, cum_T).then_inc(cum_stored, 16)
            pool.wait_ge(cum_stored, 16)

            def load_cum(h, s, first=False):
                if not first:
                    pool.wait_ge(logits, (h - 1) * NT)
                pool.dma_start(cum_row[:, s, :], cum_dram[ds(h, 1), :].broadcast_to([P, SEQ]))\
                    .then_inc(cum_loaded[s], 16)

            def head_power(h):
                pool.wait_ge(qkms_ready, h + 1)
                power(qkr[:, :, :], qkms[:, :, :], 2 * NT).then_inc(qkr_ready, 1)

            load_cum(0, 0, first=True)
            load_cum(1, 1, first=True)
            head_power(0)
            head_power(1)
            with pool.Fori(1, H // 2) as j:
                for s in range(2):
                    load_cum(j * 2 + s, s)
                    head_power(j * 2 + s)

        @block.scalar
        def _(act):
            act.dma_start(a_rows[:, :], a_norm_g[0].rearrange("(k p) -> k p", p=P))\
                .then_inc(a_rows_loaded, 16)
            act.dma_start(b_rows[:, :], b_norm_g[0].rearrange("(k p) -> k p", p=P))\
                .then_inc(b_rows_loaded, 16)
            act.wait_ge(const_ready, 4)
            act.activation(first_use[:, :], mhalf[:, 0:1], ACT.Copy)

            def split(n, q, i, first=False):
                s = i % R
                act.wait_ge(w_loaded[s], q * 16 + (i // R * 16 + 16))
                if not first:
                    act.wait_ge(tile_used, n + (i - R + 1))
                act.activation(w_hi[:, s, :], w_raw[:, s, :], ACT.Copy).then_inc(hi_ready, 1)

            def step(n, q, i):
                split(n, q, i + LEAD)

            def x_high(k, gain, done, S=1):
                act.wait_ge(xT_ready, done + k + 1)
                act.activation(xh[:, k, :], ps[S][:, k % 4, :], ACT.Copy,
                               scale=gain[:, k:k + 1]).then_inc(xh_ready, 1)

            def x_square(t, done):
                act.activation(junk, acc[:, t, :], ACT.Square, accum_out=ssx[:, t:t + 1])\
                    .then_inc(ssx_ready, 1)
                act.wait_ge(ssx_ready, done + t + 1)

            act.wait_ge(gain_ready, 1)
            for k in range(2):
                x_high(k, a_gain, 0)
                split(0, 0, k, first=True)
            split(0, 0, 2, first=True)
            for k in (2, 3):
                x_high(k, a_gain, 0)
            for k in range(KC):
                split(0, 0, k + LEAD, first=k + LEAD < R)
                if 4 <= k + 3 < KC:
                    x_high(k + 3, a_gain, 0)
                if k in (7, 9, 11, 13):
                    if k == 7:
                        for loaded in x_loaded:
                            act.wait_ge(loaded, 16)
                    x_square((k - 7) // 2, 0)

            def v_leave(n, i, S, b):
                act.wait_ge(tile_used, n + i)
                for t in range(NT):
                    act.activation(v[:, ds(b * 2, 2), t, :], ps[S][:, t, :].rearrange("p (g d) -> p g d", g=2),
                                   ACT.Gelu_apprx_tanh, scale=rstd[:, t:t + 1]).then_inc(v_out, 1)
                act.wait_ge(vsq_ready, b * NT)
                for t in range(NT):
                    act.wait_ge(v_out, b * NT + (t + 1))
                    act.activation((ug_v, zz_v)[t // 2][:, t % 2 * 2:t % 2 * 2 + 2, :], v[:, ds(b * 2, 2), t, :],
                                   ACT.Square, accum_out=vsq[:, t, ds(b, 1)]).then_inc(vsq_ready, 1)

            act.wait_ge(rstd_ready, 1)
            v_leave(0, KC, 0, 0)
            for k in range(KC):
                step(KC, KC // R, k)
            v_leave(KC, KC, 1, 1)
            with act.Fori(1, VB // 2) as j:
                for e in range(2):
                    n, q = j * (2 * KC), j * (2 * KC // R)
                    for k in range(KC):
                        step(n, q, e * KC + k)
                    v_leave(n, (e + 1) * KC, e, j * 2 + e)

            def leave(g, S):
                act.wait_ge(z_scaled, g + 1)
                act.activation(ps[S][:, OK:, :], zz[:, :, :], ACT.Tanh, scale=0.5).then_inc(tanh_ready, 1)
                act.wait_ge(u_scaled, g + 1)
                act.activation(ug[:, :, :], ug[:, :, :], ACT.Gelu_apprx_tanh).then_inc(gelu_ready, 1)

            def y_high(count, hi=yh):
                act.wait_ge(y_ready, count)
                act.activation(hi[:, :, :], ug[:, :, :], ACT.Copy).then_inc(yh_ready, 1)

            def a_block(n, q, off, g, S):
                for k in range(KC):
                    step(n, q, off + k)
                    if k == 2:
                        act.wait_ge(tile_used, n + off)
                        y_high(g)
                leave(g, S)

            def out_steps(n, q, off, inside=None):
                for i in range(OT):
                    step(n, q, off + i)
                    if inside and i == inside[0]:
                        inside[1]()

            for k in range(KC):
                step(A0, A0 // R, k)
            leave(0, 0)
            with act.Fori(0, G // 2 - 1) as j:
                n, q = j * APAIR + AL, j * (APAIR // R) + AL // R
                a_block(n, q, 0, j * 2 + 1, 1)
                out_steps(n, q, KC)
                a_block(n, q, KC + OT, j * 2 + 2, 0)
                out_steps(n, q, 2 * KC + OT)
            a_block(AE, AE // R, 0, G - 1, 1)
            out_steps(AE, AE // R, KC, (4, lambda: y_high(G, y_last)))
            out_steps(AE, AE // R, KC + OT, (OT - 2, lambda: [x_high(k, b_gain, KC, 0) for k in range(4)]))

            act.wait_ge(y_ready, G)
            for k in range(KC):
                step(B0, B0 // R, k)
                if k + 4 < KC:
                    x_high(k + 4, b_gain, KC)
                if k in (3, 5, 7, 9):
                    x_square((k - 3) // 2, NT)
                elif k == 10:
                    act.wait_ge(wf_loaded, 16)
                    act.activation(wf_hi, wf_raw, ACT.Copy).then_inc(wf_hi_ready, 1)
                elif k == 13:
                    act.wait_ge(f_step, 2)
                    act.activation(f_abs, f_lin, ACT.Abs, bias=fb_col[0:H, :]).then_inc(f_act, 1)
                    act.wait_ge(f_act, 1)
                    act.activation(f_abs, f_abs, ACT.Exp, scale=-1.0).then_inc(f_act, 1)
                    act.wait_ge(f_act, 2)
                    act.activation(f_abs, f_abs, ACT.Ln, bias=1.0).then_inc(f_act, 1)

            def head_leave(n, i, h, S):
                act.wait_ge(tile_used, n + i)
                act.wait_ge(yb_ready, h)
                for t in range(NT):
                    ins = act.activation(zb[:, t, :], ps[S][:, t, 3 * HD:4 * HD], ACT.Tanh,
                                         scale=hrstd[:, t:t + 1])
                ins.then_inc(tanh_b, 1)
                for t in range(NT):
                    ins = act.activation(vn[:, t, :], ps[S][:, t, 2 * HD:3 * HD], ACT.Copy,
                                         scale=rstd[:, t:t + 1])
                ins.then_inc(v_b, 1)

            def head_squares(h):
                act.wait_ge(qk_out, h + 1)
                act.wait_ge(probsT_psum, h)
                for t in range(NT):
                    for s in range(2):
                        ins = act.activation(probs[:, (2 * t + s) * P:(2 * t + s + 1) * P], qk[:, t, s, :],
                                             ACT.Square, scale=rstd[:, t:t + 1],
                                             accum_out=qkss[:, t, s:s + 1])
                ins.then_inc(qkss_ready, 1)

            def q_turned(h, O):
                act.wait_ge(qkT_psum, h * 2 + 1)
                act.activation(qT, ps[O][:, 0, :], ACT.Copy).then_inc(qT_ready, 1)

            def exps(h):
                for i in range(NT):
                    act.wait_ge(nmax_ready, h * NT + (i + 1))
                    act.activation(probs[:, row_at[i]:row_at[i + 1]], probs[:, row_at[i]:row_at[i + 1]],
                                   ACT.Exp, bias=nmax[:, i:i + 1], accum_out=rsum[:, i:i + 1])\
                        .then_inc(probs_ready, 1)

            def probs_turned(h, O):
                act.wait_ge(probsT_psum, h + 1)
                act.activation(probs_T[:, 0:8 * P].rearrange("p (b c) -> p b c", b=2),
                               ps[O][:, 0:2, :], ACT.Copy).then_inc(probsT_act, 1)

            def y_turned(h, O, hi):
                act.wait_ge(yT_psum, h + 1)
                act.activation(hi, ps[O][:, 0, :], ACT.Copy).then_inc(yh_ready, 1)

            def b_block(n, q, off, h, S, hi):
                for k in range(KC):
                    step(n, q, off + k)
                    if k == 1:
                        head_squares(h - 1)
                    elif k == 3:
                        q_turned(h - 1, 1 - S)
                    elif k == 6:
                        exps(h - 1)
                    elif k == 8:
                        probs_turned(h - 1, 1 - S)
                    elif k == 12:
                        y_turned(h - 1, 1 - S, hi)
                head_leave(n, off + KC, h, S)

            act.wait_ge(rstd_ready, 2)
            act.wait_ge(hrstd_ready, 2)
            head_leave(B0, KC, 0, 0)
            with act.Fori(0, H // 2 - 2) as j:
                n, q = j * BPAIR + BL, j * (BPAIR // R) + BL // R
                b_block(n, q, 0, j * 2 + 1, 1, yh[:, 0, :])
                b_block(n, q, KC, j * 2 + 2, 0, yh[:, 1, :])
                for i in range(OT):
                    step(n, q, 2 * KC + i)
            q = BE // R
            b_block(BE, q, 0, H - 3, 1, yh[:, 0, :])
            b_block(BE, q, KC, H - 2, 0, yh[:, 1, :])
            b_block(BE, q, 2 * KC, H - 1, 1, xh[:, 0, :])
            for i in range(LAST - LEAD):
                step(BE, q, 3 * KC + i)
                if i == 1:
                    head_squares(H - 1)
                elif i == 4:
                    q_turned(H - 1, 0)
                elif i == 5:
                    exps(H - 1)
                elif i == 7:
                    probs_turned(H - 1, 0)
                elif i == 9:
                    y_turned(H - 1, 0, xh[:, 1, :])

        @block.tensor
        def _(pe):
            def tile(n, i, S, hi, lo, start, stop):
                s = i % R
                pe.wait_ge(lo_ready, n + (i + 1))
                for t in range(NT):
                    a, b = hi[:, t * P:(t + 1) * P], lo[:, t * P:(t + 1) * P]
                    pe.matmul(ps[S][:, t, :], a, w_hi[:, s, :], start=start, stop=False)
                    pe.matmul(ps[S][:, t, :], a, w_lo[:, s, :], start=False, stop=False)
                    mm = pe.matmul(ps[S][:, t, :], b, w_hi[:, s, :], start=False, stop=stop)
                mm.then_inc(tile_used, 1)

            def in_tile(n, i, k, S):
                tile(n, i, S, xh[:, k, :], xl[:, k, :], k == 0, k == KC - 1)

            def in_tile_fm(n, i, k, S):
                s = i % R
                pe.wait_ge(lo_ready, n + (i + 1))
                for f in range(FB // P):
                    a, b = w_hi[:, s, f * P:(f + 1) * P], w_lo[:, s, f * P:(f + 1) * P]
                    pe.matmul(ps[S][:, f, :], a, xh[:, k, :], start=(k == 0), stop=False)
                    pe.matmul(ps[S][:, f, :], a, xl[:, k, :], start=False, stop=False)
                    mm = pe.matmul(ps[S][:, f, :], b, xh[:, k, :], start=False, stop=(k == KC - 1))
                mm.then_inc(tile_used, 1)

            def turn_x(k, done, S=1):
                if k >= 4:
                    pe.wait_ge(xl_ready, done + k - 3)
                for t in range(NT):
                    mm = pe.transpose(ps[S][:, k % 4, t * P:(t + 1) * P],
                                      acc[:, t, k * P:(k + 1) * P], ident[:, :])
                mm.then_inc(xT_ready, 1)

            pe.wait_ge(const_ready, 7)
            pe.wait_ge(a_rows_loaded, 16)
            pe.transpose(ps[0][:, 0, 0:KC], a_rows[:, :], ident[0:KC, 0:KC]).then_inc(rows_T, 1)
            for k in range(2):
                pe.wait_ge(x_loaded[k], 16)
                turn_x(k, 0)
            pe.wait_ge(b_rows_loaded, 16)
            pe.transpose(ps[0][:, 1, 0:KC], b_rows[:, :], ident[0:KC, 0:KC]).then_inc(rows_T, 1)
            pe.wait_ge(gain_ready, 2)
            for k in range(KC):
                pe.wait_ge(xl_ready, k + 1)
                in_tile(0, k, k, 0)
                for c in (2, 3) if k == 0 else (k + 3,):
                    if c < KC:
                        if c < X1:
                            pe.wait_ge(x_loaded[c], 16)
                        elif c % X1 == 0:
                            pe.wait_ge(x_loaded[X1 + c // X1 - 1], 16)
                        turn_x(c, 0)
            for k in range(KC):
                in_tile(KC, k, k, 1)
            with pe.Fori(1, VB // 2) as j:
                for S in range(2):
                    pe.wait_ge(v_out, j * (2 * NT) + (S * NT - NT))
                    for k in range(KC):
                        in_tile(j * (2 * KC), S * KC + k, k, S)

            def turn_ws(g, s, O):
                pe.wait_ge(ws_masked, g + 1)
                pe.transpose(ps[O][:, 3, 0:P], ws_raw[:, s, :], ident[:, :]).then_inc(ws_T_psum, 1)

            def mix(g, O):
                pe.wait_ge(ws_T_ready, g + 1)
                pe.wait_ge(v_normed, g + 1)
                for f in range(OK):
                    for c in range(NT):
                        mm = pe.matmul(ps[O][:, 2 + f, c * P:(c + 1) * P], zz_v[:, c, f * P:(f + 1) * P],
                                       ws_T[:, :], start=True, stop=True)
                mm.then_inc(mixed, 1)

            def a_block(n, off, g, S):
                O = 1 - S
                pe.wait_ge(sum_out, g * NF - 1)
                pe.wait_ge(mix_ready, g)
                for k in range(KC):
                    in_tile_fm(n, off + k, k, S)
                    if k == 3:
                        pe.wait_ge(sum_out, g * NF)
                        pe.wait_ge(block_out, g)
                        turn_ws(g, S, O)
                    elif k == 8:
                        mix(g, O)

            def out_proj(n, off, sets, hi, lo, gates, inside={}):
                for f in range(NF):
                    for gate in gates[f]:
                        pe.wait_ge(*gate)
                    for k in range(OK):
                        tile(n, off + f * OK + k, sets[f], hi[:, k, :], lo[:, k, :], k == 0, k == OK - 1)
                        if f * OK + k in inside:
                            inside[f * OK + k]()

            def a_out(n, off, g, S, count, leaves, inside={}, hi=yh, lo=yl):
                out_proj(n, off, [1 - S, S, 1 - S, S], hi, lo,
                         [[(yl_ready, count)],
                          [leaves],
                          [(sum_out, g * NF + 1)],
                          [(sum_out, g * NF + 2)]],
                         inside)

            pe.wait_ge(v_out, NT * (VB - 1))
            for k in range(KC):
                in_tile_fm(A0, k, k, 0)
                if k == 3:
                    pe.wait_ge(v_out, NT * VB)
                    turn_ws(0, 0, 1)
                    for t in range(NT):
                        mm = pe.transpose(ps[1][:, 0, t * P:(t + 1) * P],
                                          rstd[:, t:t + 1].broadcast_to([P, P]), ident[:, :])
                    mm.then_inc(bc_psum, 1)
                elif k == 8:
                    mix(0, 1)
            with pe.Fori(0, G // 2 - 1) as j:
                n = j * APAIR + AL
                for e in range(2):
                    g, S, off = j * 2 + (e + 1), 1 - e, e * (KC + OT)
                    a_block(n, off, g, S)
                    pe.wait_ge(mix_ready, g + 1)
                    a_out(n, off + KC, g, S, g, (block_out, g + 1))
            g = G - 1
            a_block(AE, 0, g, 1)
            pe.wait_ge(mix_ready, g + 1)

            def turn_first_x():
                pe.wait_ge(sum_out, G * NF + 3)
                for k in range(4):
                    turn_x(k, KC, 0)

            a_out(AE, KC, g, 1, g, (block_out, g + 1))
            pe.wait_ge(sum_out, g * NF + 3)
            a_out(AE, KC + OT, G, 1, G, (sum_out, g * NF + 4), {OT - 2: turn_first_x}, y_last, y_last_lo)

            S0 = NF * (G + 1)
            for k in range(KC):
                pe.wait_ge(xl_ready, KC + max(k + 1, 4))
                in_tile(B0, k, k, 0)
                if k == 0:
                    pe.wait_ge(sum_out, S0)
                if k + 4 < KC:
                    turn_x(k + 4, KC)
                if k == 12:
                    pe.wait_ge(xl_ready, 2 * KC)
                    pe.wait_ge(rstd_ready, 2)
                    for t in range(NT):
                        mm = pe.transpose(ps[1][0:H, 1, t * P:(t + 1) * P],
                                          rstd[:, t:t + 1].broadcast_to([P, H]), ident[:, :])
                    mm.then_inc(rstdT_psum, 1)
                    pe.wait_ge(wf_lo_ready, 1)
                    for c in range(KC):
                        f_hi, f_lo = wf_hi[:, c * H:(c + 1) * H], wf_lo[:, c * H:(c + 1) * H]
                        o = ps[1][0:H, 0, :]
                        pe.matmul(o, f_hi, xh[:, c, :], start=(c == 0), stop=False)
                        pe.matmul(o, f_hi, xl[:, c, :], start=False, stop=False)
                        mm = pe.matmul(o, f_lo, xh[:, c, :], start=False, stop=(c == KC - 1))
                    mm.then_inc(f_psum, 1)
            pe.wait_ge(cumT_ready, 1)
            for t in range(NT):
                mm = pe.transpose(ps[1][:, 2, t * H:(t + 1) * H], cum_T[:, t * P:(t + 1) * P],
                                  ident[0:H, 0:H])
            mm.then_inc(cumc_psum, 1)

            def turn_qk(h, O):
                pe.wait_ge(heads_out, h + 1)
                pe.wait_ge(qk_normed, h + 1)
                for s in range(2):
                    for t in range(NT):
                        mm = pe.transpose(ps[O][:, s, t * P:(t + 1) * P], qk[:, t, s, :], ident[:, :])
                    mm.then_inc(qkT_psum, 1)

            def score(h, O):
                pe.wait_ge(qT_ready, h + 1)
                pe.wait_ge(kT_ready, h + 1)
                for i in range(NT):
                    pe.matmul(ps[O][:, i, 0:(i + 1) * P], qT[:, i * P:(i + 1) * P],
                              kT[:, 0:(i + 1) * P], start=True, stop=False)
                    pe.matmul(ps[O][:, i, i * P:(i + 1) * P], ident_b[:, :], mask_b[:, :],
                              start=False, stop=True).then_inc(scores, 1)

            def turn_probs(h, O):
                pe.wait_ge(probs_ready, h * NT + NT)
                for b in range(NB):
                    mm = pe.transpose(ps[O][:, b // 4, b % 4 * P:(b % 4 + 1) * P],
                                      probs[:, b * P:(b + 1) * P], ident[:, :])
                mm.then_inc(probsT_psum, 1)

            def attend(h, O):
                pe.wait_ge(probsT_act, h + 1)
                pe.wait_ge(probsT_dve, h + 1)
                for i in range(NT):
                    for c in range(i + 1):
                        b = row_at[i] + c * P
                        mm = pe.matmul(ps[O][:, 3, i * P:(i + 1) * P], probs_T[:, b:b + P],
                                       vn[:, c, :], start=(c == 0), stop=(c == i))
                mm.then_inc(attended, 1)

            def turn_yb(h, O):
                pe.wait_ge(yb_ready, h + 1)
                for t in range(NT):
                    mm = pe.transpose(ps[O][:, 0, t * P:(t + 1) * P], yb[:, t, :], ident[:, :])
                mm.then_inc(yT_psum, 1)

            def b_block(n, off, h, S, added=None):
                for k in range(KC):
                    in_tile(n, off + k, k, S)
                    if k == 3 and added is not None:
                        pe.wait_ge(sum_out, added)
                    elif k == 4:
                        turn_qk(h - 1, 1 - S)
                    elif k == 6:
                        score(h - 1, 1 - S)
                    elif k == 9:
                        turn_probs(h - 1, 1 - S)
                    elif k == 11:
                        attend(h - 1, 1 - S)
                    elif k == 13:
                        turn_yb(h - 1, 1 - S)

            pe.wait_ge(cumc_ready, 1)
            with pe.Fori(0, H // 2 - 2) as j:
                n = j * BPAIR + BL
                pe.wait_ge(sum_out, j * NF + (S0 - 1))
                b_block(n, 0, j * 2 + 1, 1, added=j * NF + S0)
                pe.wait_ge(yl_ready, j * 2 + (G + 1))
                b_block(n, KC, j * 2 + 2, 0)
                out_proj(n, 2 * KC, [1, 0, 1, 0], yh, yl,
                         [[(yl_ready, j * 2 + (G + 2))],
                          [(heads_out, j * 2 + 3)],
                          [(sum_out, j * NF + (S0 + 1))],
                          [(sum_out, j * NF + (S0 + 2))]])
            S1 = S0 + (H // 2 - 2) * NF
            pe.wait_ge(sum_out, S1 - 1)
            b_block(BE, 0, H - 3, 1, added=S1)
            pe.wait_ge(yl_ready, G + H - 3)
            b_block(BE, KC, H - 2, 0)
            pe.wait_ge(yl_ready, G + H - 2)
            b_block(BE, 2 * KC, H - 1, 1)
            y_of = {H - 4: (yh, yl, 0), H - 3: (yh, yl, 1), H - 2: (xh, xl, 0), H - 1: (xh, xl, 1)}
            i = 0
            for b, (f, S, heads) in enumerate(LAST_BLOCKS):
                if b == 0:
                    pe.wait_ge(yl_ready, G + H - 1)
                elif b == 1:
                    pe.wait_ge(heads_out, H)
                before = {2: 1, 3: 2, 4: 3, 6: 4, 7: 5}.get(b)
                for h in heads:
                    if h == H - 1:
                        pe.wait_ge(yl_ready, G + H)
                    s, n = (3 * KC + i) % R, BE + 3 * KC + i
                    pe.wait_ge(lo_ready, n + 1)
                    hi, lo, c = y_of[h]
                    for t in range(NT):
                        if h == heads[0] and before is not None:
                            pe.wait_ge(bank_added, before * NT + t + 1)
                        a, d = hi[:, c, t * P:(t + 1) * P], lo[:, c, t * P:(t + 1) * P]
                        pe.matmul(ps[S][:, t, :], a, w_hi[:, s, :], start=(h == heads[0]), stop=False)
                        pe.matmul(ps[S][:, t, :], a, w_lo[:, s, :], start=False, stop=False)
                        mm = pe.matmul(ps[S][:, t, :], d, w_hi[:, s, :], start=False,
                                       stop=(h == heads[-1]))
                        if h == heads[-1] and t < NT - 1:
                            mm.then_inc(bank_done, 1)
                    mm.then_inc(tile_used, 1)
                    if i == 4:
                        pe.wait_ge(bank_added, NT)
                        turn_qk(H - 1, 0)
                    elif i == 5:
                        score(H - 1, 0)
                    elif i == 7:
                        turn_probs(H - 1, 0)
                    elif i == 8:
                        attend(H - 1, 0)
                    elif i == 9:
                        turn_yb(H - 1, 0)
                    i += 1

        @block.vector
        def _(dve):
            def split(n, i):
                s = i % R
                dve.wait_ge(hi_ready, n + (i + 1))
                dve.tensor_tensor(w_lo[:, s, :], w_raw[:, s, :], w_hi[:, s, :].bitcast(F32),
                                  ALU.subtract).then_inc(lo_ready, 1)

            def step(n, i):
                split(n, i + LEAD)

            def x_low(k, gain, done, S=1):
                dve.wait_ge(xh_ready, done + k + 1)
                dve.scalar_tensor_tensor(xl[:, k, :], ps[S][:, k % 4, :], gain[:, k:k + 1],
                                         xh[:, k, :].bitcast(F32), ALU.mult, ALU.subtract)\
                    .then_inc(xl_ready, 1)

            def x_stats(layer):
                dve.wait_ge(ssx_ready, (layer + 1) * NT)
                dve.tensor_scalar(msx[:, :], ssx[:, :], 1.0 / D, EPS, ALU.mult, ALU.add)\
                    .then_inc(msx_ready, 1)
                dve.wait_ge(rstd_ready, layer + 1)
                dve.tensor_scalar(hrstd[:, :], rstd[:, :], 0.5, None, ALU.mult).then_inc(hrstd_ready, 1)

            dve.wait_ge(rows_T, 1)
            dve.tensor_copy(a_gain[:, :], ps[0][:, 0, 0:KC]).then_inc(gain_ready, 1)
            dve.wait_ge(gain_ready, 1)
            x_low(0, a_gain, 0)
            split(0, 0)
            dve.wait_ge(rows_T, 2)
            dve.tensor_copy(b_gain[:, :], ps[0][:, 1, 0:KC]).then_inc(gain_ready, 1)
            x_low(1, a_gain, 0)
            split(0, 1)
            split(0, 2)
            for k in (2, 3):
                x_low(k, a_gain, 0)
            for k in range(KC):
                step(0, k)
                if 4 <= k + 3 < KC:
                    x_low(k + 3, a_gain, 0)
            x_stats(0)
            for k in range(KC):
                step(KC, k)
            with dve.Fori(1, VB // 2) as j:
                for k in range(2 * KC):
                    step(j * (2 * KC), k)

            def v_norm(g):
                dve.wait_ge(vg_loaded, g * 16 + 16)
                for c in range(NT):
                    v_c = v[:, ds(g, 1), c, :].rearrange("p g d -> p (g d)")
                    ins = dve.scalar_tensor_tensor(zz_v[:, c, :], v_c, vrstd[:, c:c + 1], vg_row[:, :],
                                                   ALU.mult, ALU.mult)
                ins.then_inc(v_normed, 1)

            def ws_leave(g, O):
                dve.wait_ge(ws_T_psum, g + 1)
                dve.tensor_copy(ws_T[:, :], ps[O][:, 3, 0:P]).then_inc(ws_T_ready, 1)

            def mix_leave(g, O):
                dve.wait_ge(mixed, g + 1)
                dve.wait_ge(bs_loaded, g * 16 + 16)
                dve.tensor_tensor(v[:, ds(g, 1), :, :].rearrange("p g c (h t) -> p (g c h) t", t=P),
                                  ps[O][:, 2:4, :].rearrange("p b (c t) -> p (b c) t", t=P),
                                  bs_row[:, :].unsqueeze(1).broadcast_to([P, OK * NT, P]), ALU.add)\
                    .then_inc(mix_ready, 1)

            def y_low(count, hi=yh, lo=yl):
                dve.wait_ge(yh_ready, count)
                dve.tensor_tensor(lo[:, :, :], ug[:, :, :], hi[:, :, :].bitcast(F32),
                                  ALU.subtract).then_inc(yl_ready, 1)

            def leave(n, i, g, S):
                factors = rstd_bc[:, :].unsqueeze(1).broadcast_to([P, OK, SEQ])
                dve.wait_ge(tile_used, n + i)
                dve.tensor_tensor(zz[:, :, :], ps[S][:, OK:, :], factors, ALU.mult).then_inc(z_scaled, 1)
                dve.tensor_tensor(ug[:, :, :], ps[S][:, 0:OK, :], factors, ALU.mult).then_inc(u_scaled, 1)
                dve.wait_ge(tanh_ready, g + 1)
                dve.scalar_tensor_tensor(zz[:, :, :], ps[S][:, OK:, :], 1.0, zz[:, :, :],
                                         ALU.add, ALU.mult).then_inc(block_out, 1)
                dve.wait_ge(gelu_ready, g + 1)
                dve.wait_ge(mix_ready, g + 1)
                dve.tensor_tensor(ug[:, :, :], ug[:, :, :],
                                  v[:, ds(g, 1), :, :].rearrange("p g (b c) d -> p (g b) (c d)", b=OK),
                                  ALU.mult).then_inc(gate_step, 1)
                dve.wait_ge(gate_step, g + 1)
                dve.wait_ge(block_out, g + 1)
                dve.scalar_tensor_tensor(ug[:, :, :], ug[:, :, :], 0.5, zz[:, :, :],
                                         ALU.mult, ALU.mult).then_inc(y_ready, 1)

            def a_block(n, off, g, S):
                for k in range(KC):
                    step(n, off + k)
                    if k == 0:
                        dve.wait_ge(y_ready, g)
                        v_norm(g)
                    elif k == 2:
                        ws_leave(g, 1 - S)
                        y_low(g)
                    elif k == 7:
                        mix_leave(g, 1 - S)
                leave(n, off + KC, g, S)

            def add_out(n, i, f, S):
                dve.wait_ge(tile_used, n + i)
                for b in range(2):
                    o = acc[:, 2 * b:2 * b + 2, f * FB:(f + 1) * FB]
                    ins = dve.tensor_tensor(o, ps[S][:, 2 * b:2 * b + 2, :], o, ALU.add)
                ins.then_inc(sum_out, 1)

            def out_steps(n, off, sets, inside=None):
                for i in range(OT):
                    step(n, off + i)
                    if inside and i == inside[0]:
                        inside[1]()
                    if i % OK == OK - 1:
                        add_out(n, off + i + 1, i // OK, sets[i // OK])

            for k in range(KC):
                step(A0, k)
                if k == 1:
                    dve.wait_ge(vsq_ready, NT * VB)
                    dve.tensor_reduce(vms[:, 0, :], vsq[:, :, :], AX.X, ALU.add).then_inc(vms_ready, 1)
                    dve.wait_ge(vms_ready, 1)
                    dve.tensor_scalar(vms[:, 1, :], vms[:, 0, :], 1.0 / AW, EPS, ALU.mult, ALU.add)\
                        .then_inc(vms_ready, 1)
                elif k == 2:
                    ws_leave(0, 1)
                    dve.wait_ge(bc_psum, 1)
                    dve.tensor_copy(rstd_bc[:, :], ps[1][:, 0, :]).then_inc(bc_ready, 1)
                elif k == 4:
                    dve.wait_ge(vrstd_ready, 1)
                    v_norm(0)
                elif k == 7:
                    dve.wait_ge(v_out, NT * VB)
                    dve.tensor_copy(vms[:, 0, :], vrstd[:, :]).then_inc(sum_out, NF)
                    mix_leave(0, 1)
            dve.wait_ge(bc_ready, 1)
            leave(A0, KC, 0, 0)
            with dve.Fori(0, G // 2 - 1) as j:
                n = j * APAIR + AL
                a_block(n, 0, j * 2 + 1, 1)
                out_steps(n, KC, [0, 1, 0, 1])
                a_block(n, KC + OT, j * 2 + 2, 0)
                out_steps(n, 2 * KC + OT, [1, 0, 1, 0])
            a_block(AE, 0, G - 1, 1)
            out_steps(AE, KC, [0, 1, 0, 1], (4, lambda: y_low(G, y_last, y_last_lo)))
            out_steps(AE, KC + OT, [0, 1, 0, 1], (OT - 2, lambda: [x_low(k, b_gain, KC, 0) for k in range(4)]))

            for k in range(KC):
                step(B0, k)
                if k + 4 < KC:
                    x_low(k + 4, b_gain, KC)
                if k == 10:
                    dve.wait_ge(wf_hi_ready, 1)
                    dve.tensor_tensor(wf_lo, wf_raw, wf_hi.bitcast(F32), ALU.subtract)\
                        .then_inc(wf_lo_ready, 1)
                elif k == 11:
                    x_stats(1)
                    dve.wait_ge(gains_loaded, 48)
                    dve.tensor_scalar(qg_row, qg_row, SCALE, None, ALU.mult).then_inc(gains_ready, 1)
                elif k == 13:
                    dve.wait_ge(rstdT_psum, 1)
                    dve.tensor_copy(rstd_row, ps[1][0:H, 1, :]).then_inc(f_step, 1)
                    dve.wait_ge(f_psum, 1)
                    dve.wait_ge(f_step, 1)
                    dve.tensor_tensor(f_lin, ps[1][0:H, 0, :], rstd_row, ALU.mult).then_inc(f_step, 1)
                    dve.wait_ge(f_step, 2)
                    dve.tensor_scalar(f_min, f_lin, fb_col[0:H, :], 0.0, ALU.add, ALU.min)\
                        .then_inc(f_step, 1)
                elif k == 14:
                    dve.wait_ge(f_act, 3)
                    dve.wait_ge(f_step, 3)
                    dve.tensor_tensor(f_log, f_min, f_abs, ALU.subtract).then_inc(f_step, 1)
                    dve.wait_ge(f_step, 4)
                    dve.wait_ge(const_ready, 8)
                    dve.tensor_tensor_scan(cum_T, f_one, f_log, 0.0, ALU.mult, ALU.add)\
                        .then_inc(cumT_ready, 1)
            dve.wait_ge(cumc_psum, 1)
            dve.tensor_copy(cum_col[:, :, :], ps[1][:, 2, 0:NT * H].rearrange("p (t h) -> p t h", t=NT))\
                .then_inc(cumc_ready, 1)
            dve.wait_ge(cumc_ready, 1)
            dve.wait_ge(gains_ready, 1)

            def head_leave(n, i, h, S):
                dve.wait_ge(tile_used, n + i)
                dve.wait_ge(tanh_b, h + 1)
                dve.wait_ge(v_b, h + 1)
                dve.tensor_copy(qk[:, :, :, :].rearrange("p t s d -> p t (s d)"),
                                ps[S][:, :, 0:2 * HD]).then_inc(qk_out, 1)
                dve.scalar_tensor_tensor(zb[:, :, :], zb[:, :, :], 1.0, ps[S][:, :, 3 * HD:4 * HD],
                                         ALU.add, ALU.mult).then_inc(heads_out, 1)

            def head_means(h):
                dve.wait_ge(qkss_ready, h + 1)
                dve.tensor_scalar(qkms[:, :, :], qkss[:, :, :], 1.0 / HD, EPS, ALU.mult, ALU.add)\
                    .then_inc(qkms_ready, 1)

            def head_norm(h):
                dve.wait_ge(qkr_ready, h + 1)
                for s in range(2):
                    ins = dve.tensor_tensor(qkr[:, :, s], qkr[:, :, s], rstd[:, :], ALU.mult)
                ins.then_inc(qkr_scaled, 1)
                dve.wait_ge(qkr_scaled, h + 1)
                for t in range(NT):
                    for s, g in ((0, qg_row), (1, kg_row)):
                        ins = dve.scalar_tensor_tensor(qk[:, t, s, :], qk[:, t, s, :], qkr[:, t, s:s + 1], g,
                                                       ALU.mult, ALU.mult)
                ins.then_inc(qk_normed, 1)

            def k_turned(h, O):
                dve.wait_ge(qkT_psum, h * 2 + 2)
                dve.tensor_copy(kT, ps[O][:, 1, :]).then_inc(kT_ready, 1)

            def row_logits(h, i, O, s):
                dve.wait_ge(scores, h * NT + (i + 1))
                p = probs[:, row_at[i]:row_at[i + 1]]
                dve.scalar_tensor_tensor(p, ps[O][:, i, 0:(i + 1) * P],
                                         cum_col[:, i, ds(h, 1)], cum_row[:, s, 0:(i + 1) * P],
                                         ALU.add, ALU.subtract).then_inc(logits, 1)
                dve.wait_ge(logits, h * NT + (i + 1))
                dve.tensor_reduce(nmax[:, i:i + 1], p, AX.X, ALU.max, negate=True).then_inc(nmax_ready, 1)

            def probs_turned(h, O):
                dve.wait_ge(probsT_psum, h + 1)
                dve.tensor_copy(probs_T[:, 8 * P:NB * P], ps[O][:, 2, 0:(NB - 8) * P])\
                    .then_inc(probsT_dve, 1)
                dve.wait_ge(probs_ready, h * NT + NT)
                dve.reciprocal(rsum[:, :], rsum[:, :]).then_inc(rinv_ready, 1)
                dve.wait_ge(rinv_ready, h * 2 + 1)
                dve.tensor_tensor(rinv[:, :], rsum[:, :], hrstd[:, :], ALU.mult).then_inc(rinv_ready, 1)

            def gate_head(h, O):
                dve.wait_ge(attended, h + 1)
                dve.wait_ge(rinv_ready, h * 2 + 2)
                for i in range(NT):
                    ins = dve.scalar_tensor_tensor(yb[:, i, :], ps[O][:, 3, i * P:(i + 1) * P],
                                                   rinv[:, i:i + 1], zb[:, i, :], ALU.mult, ALU.mult)
                ins.then_inc(yb_ready, 1)

            def y_turned(h, O, hi, lo):
                dve.wait_ge(yh_ready, h + (G + 1))
                dve.tensor_tensor(lo, ps[O][:, 0, :], hi.bitcast(F32), ALU.subtract).then_inc(yl_ready, 1)

            def b_block(n, off, h, S, s, loads, hi, lo):
                for k in range(KC):
                    step(n, off + k)
                    if k == 1:
                        head_means(h - 1)
                    elif k == 2:
                        head_norm(h - 1)
                    elif k == 3:
                        k_turned(h - 1, 1 - S)
                    elif k == 5:
                        dve.wait_ge(cum_loaded[s], loads)
                        row_logits(h - 1, 0, 1 - S, s)
                        row_logits(h - 1, 1, 1 - S, s)
                    elif k == 6:
                        row_logits(h - 1, 2, 1 - S, s)
                        row_logits(h - 1, 3, 1 - S, s)
                    elif k == 8:
                        probs_turned(h - 1, 1 - S)
                    elif k == 10:
                        gate_head(h - 1, 1 - S)
                    elif k == 12:
                        y_turned(h - 1, 1 - S, hi, lo)
                head_leave(n, off + KC, h, S)

            y0, y1 = (yh[:, 0, :], yl[:, 0, :]), (yh[:, 1, :], yl[:, 1, :])
            head_leave(B0, KC, 0, 0)
            with dve.Fori(0, H // 2 - 2) as j:
                n = j * BPAIR + BL
                b_block(n, 0, j * 2 + 1, 1, 0, j * 16 + 16, *y0)
                b_block(n, KC, j * 2 + 2, 0, 1, j * 16 + 16, *y1)
                for i in range(OT):
                    step(n, 2 * KC + i)
                    if i % OK == OK - 1:
                        add_out(n, 2 * KC + i + 1, i // OK, (1, 0, 1, 0)[i // OK])
            b_block(BE, 0, H - 3, 1, 0, 8 * (H - 2), *y0)
            b_block(BE, KC, H - 2, 0, 1, 8 * (H - 2), *y1)
            b_block(BE, 2 * KC, H - 1, 1, 0, 8 * H, xh[:, 0, :], xl[:, 0, :])

            def add_last(b, f, S, tiles):
                for t in range(NT):
                    if t < NT - 1:
                        dve.wait_ge(bank_done, b * (NT - 1) + t + 1)
                    else:
                        dve.wait_ge(tile_used, BE + 3 * KC + tiles)
                    o = acc[:, t, f * FB:(f + 1) * FB]
                    dve.tensor_tensor(o, ps[S][:, t, :], o, ALU.add).then_inc(bank_added, 1)

            ends = {}
            for b, (f, S, heads) in enumerate(LAST_BLOCKS):
                ends[sum(len(c[2]) for c in LAST_BLOCKS[:b + 1]) - 1] = (b, f, S)
            for i in range(LAST):
                if i < LAST - LEAD:
                    step(BE, 3 * KC + i)
                if i in ends:
                    add_last(*ends[i], i + 1)
                if i == 1:
                    head_means(H - 1)
                elif i == 2:
                    head_norm(H - 1)
                elif i == 4:
                    k_turned(H - 1, 0)
                elif i == 5:
                    dve.wait_ge(cum_loaded[1], 8 * H)
                    for r in range(NT):
                        row_logits(H - 1, r, 0, 1)
                elif i == 7:
                    probs_turned(H - 1, 0)
                elif i == 8:
                    gate_head(H - 1, 0)
                elif i == 9:
                    y_turned(H - 1, 0, xh[:, 1, :], xl[:, 1, :])


_INS = ["x", "a_norm_g", "a_w_in", "a_v_norm_g", "a_w_s", "a_b_s", "a_w_out",
        "b_norm_g", "b_w_in", "b_f_bias", "b_q_norm_g", "b_k_norm_g", "b_w_out"]


def kernel(**inputs):
    import numpy as _np
    import concourse.bacc as _bacc
    from concourse import mybir as _mybir
    from concourse.bass_utils import run_bass_kernel_spmd as _run

    nc = _bacc.Bacc("TRN2", target_bir_lowering=False, num_devices=1)
    arrays, args = {}, []
    for name in _INS:
        a = _np.ascontiguousarray(inputs[name])
        arrays[f"in_{name}_dram"] = a
        args.append(nc.dram_tensor(f"in_{name}_dram", a.shape, _mybir.dt.from_np(a.dtype),
                                   kind="ExternalInput").ap())
    out = nc.dram_tensor("out_dram", inputs["x"].shape, _mybir.dt.float32, kind="ExternalOutput").ap()
    build_trunk(nc, *args, out)
    r = _run(nc, [arrays], core_ids=[0])
    return r.results[0]["out_dram"]
```
